# Optimizing a Trainium2 kernel written in Bass

```python
import math
import jax, jax.numpy as jnp
from jax import lax
import numpy as np

D_MODEL = 1024
BATCH = 1
SEQ = 1024
DEPTH = 1

N_HEADS = 8
N_KV_HEADS = 2
HEAD_DIM = 64
KV_REP = N_HEADS // N_KV_HEADS
Q_BLOCK = 128
ROPE_THETA = 10000.0
GRID_W = 64
ROT_HALF = HEAD_DIM // 2
SSM_WIDTH = 256
SSM_GROUP = 16
SSM_GROUPS = SSM_WIDTH // SSM_GROUP
SSM_STATE = 64
N_DIR = 2
N_EXPERTS = 64
EXPERT_DIM = 128
TOP_K = 8
N_EXPERT_GROUPS = 8
TOPK_GROUPS = 4
EXPERTS_PER_GROUP = N_EXPERTS // N_EXPERT_GROUPS
SHARED_DIM = 256
ROUTED_SCALE = 2.5
PLE_DIM = 256
EPS = 1e-6

Q_W = N_HEADS * HEAD_DIM
KV_W = N_KV_HEADS * HEAD_DIM
IN_WIDTH = Q_W + 2 * KV_W + SSM_WIDTH + 2 * D_MODEL
IN_SPLITS = (Q_W, Q_W + KV_W, Q_W + 2 * KV_W, Q_W + 2 * KV_W + SSM_WIDTH,
             Q_W + 2 * KV_W + SSM_WIDTH + D_MODEL)

kernel_name = "hybrid_gqa_s5_moe_encoder"

def rmsnorm(x, g):
    xf = x.astype(jnp.float32)
    y = xf * lax.rsqrt(jnp.mean(xf * xf, axis=-1, keepdims=True) + EPS)
    return (y * g.astype(jnp.float32)).astype(x.dtype)

def _rope_half(x, ang):
    cos = jnp.cos(ang)[None, :, None, :]
    sin = jnp.sin(ang)[None, :, None, :]
    x1, x2 = jnp.split(x, 2, axis=-1)
    return jnp.concatenate([x1 * cos - x2 * sin, x2 * cos + x1 * sin], axis=-1)

def axial_rope(x, row_ang, col_ang):
    xf = x.astype(jnp.float32)
    out = jnp.concatenate([_rope_half(xf[..., :ROT_HALF], row_ang),
                           _rope_half(xf[..., ROT_HALF:], col_ang)], axis=-1)
    return out.astype(x.dtype)

def block_attention(q, k, v):
    B, L = q.shape[0], q.shape[1]
    n_blk = L // Q_BLOCK
    scale = 1.0 / math.sqrt(HEAD_DIM)
    qb = q.reshape(B, n_blk, Q_BLOCK, N_KV_HEADS, KV_REP, HEAD_DIM).transpose(1, 0, 2, 3, 4, 5)

    def attend_block(q_blk):
        s = jnp.einsum('bqgrd,bkgd->bgrqk', q_blk, k, preferred_element_type=jnp.float32) * scale
        pr = jax.nn.softmax(s, axis=-1).astype(v.dtype)
        return jnp.einsum('bgrqk,bkgd->bqgrd', pr, v)

    ob = lax.map(attend_block, qb)
    return ob.transpose(1, 0, 2, 3, 4, 5).reshape(B, L, Q_W)

def _lin_combine(e1, e2):
    a1, b1 = e1
    a2, b2 = e2
    return a1 * a2, a2 * b1 + b2

def _s5_scan(u, a_re, a_im, log_dt, b_re, b_im, c_re, c_im):
    lam = lax.complex(a_re, a_im)
    dt = jnp.exp(log_dt)[:, None]
    a_bar = jnp.exp(lam * dt)
    b_bar = ((a_bar - 1.0) / lam)[..., None] * lax.complex(b_re, b_im)
    bu = jnp.einsum('gpc,blgc->blgp', b_bar, u.astype(jnp.complex64))
    a_seq = jnp.broadcast_to(a_bar, (1, u.shape[1]) + a_bar.shape)
    _, state = lax.associative_scan(_lin_combine, (a_seq, bu), axis=1)
    return jnp.real(jnp.einsum('gcp,blgp->blgc', lax.complex(c_re, c_im), state))

def s5_branch(u_raw, a_re, a_im, log_dt, b_re, b_im, c_re, c_im, d_skip, w_glu, b_glu):
    B, L = u_raw.shape[0], u_raw.shape[1]
    f32 = jnp.float32
    u = u_raw.astype(f32).reshape(B, L, SSM_GROUPS, SSM_GROUP)
    y = d_skip.astype(f32).reshape(SSM_GROUPS, SSM_GROUP) * u
    for d in range(N_DIR):
        args = [t[d].astype(f32) for t in (a_re, a_im, log_dt, b_re, b_im, c_re, c_im)]
        if d == 0:
            y = y + _s5_scan(u, *args)
        else:
            y = y + jnp.flip(_s5_scan(jnp.flip(u, axis=1), *args), axis=1)
    y = jax.nn.gelu(y.reshape(B, L, SSM_WIDTH))
    y = y * jax.nn.sigmoid(y @ w_glu.astype(f32) + b_glu.astype(f32))
    return y.astype(u_raw.dtype)

def moe(xn, w_router, router_bias, w_exp_gate, w_exp_up, w_exp_down, w_sh_gate, w_sh_up, w_sh_down):
    B, L, D = xn.shape
    f32 = jnp.float32
    xf = xn.reshape(B * L, D)
    scores = jax.nn.sigmoid(jnp.dot(xf, w_router, preferred_element_type=f32))
    biased = scores + router_bias.astype(f32)
    grp = biased.reshape(-1, N_EXPERT_GROUPS, EXPERTS_PER_GROUP)
    grp_score = jnp.sum(lax.top_k(grp, 2)[0], axis=-1)
    _, grp_idx = lax.top_k(grp_score, TOPK_GROUPS)
    grp_mask = jnp.sum(jax.nn.one_hot(grp_idx, N_EXPERT_GROUPS, dtype=f32), axis=1)
    exp_mask = jnp.repeat(grp_mask, EXPERTS_PER_GROUP, axis=-1) > 0.0
    masked = jnp.where(exp_mask, biased, -1e30)
    _, top_idx = lax.top_k(masked, TOP_K)
    top_w = jnp.take_along_axis(scores, top_idx, axis=-1)
    top_w = top_w / jnp.sum(top_w, axis=-1, keepdims=True) * ROUTED_SCALE
    gates = jnp.einsum('nk,nke->en', top_w,
                       jax.nn.one_hot(top_idx, N_EXPERTS, dtype=f32)).astype(xn.dtype)

    def expert_step(acc, ew):
        wg, wu, wd, g = ew
        hid = jax.nn.silu(xf @ wg) * (xf @ wu)
        return acc + (hid * g[:, None]) @ wd, None

    routed, _ = lax.scan(expert_step, jnp.zeros_like(xf), (w_exp_gate, w_exp_up, w_exp_down, gates))
    shared = (jax.nn.silu(xf @ w_sh_gate) * (xf @ w_sh_up)) @ w_sh_down
    return (routed + shared).reshape(B, L, D)

def setup_inputs(seed: int = 0) -> dict:
    key = jax.random.key(seed)
    ks = jax.random.split(key, 40)
    nrm = jax.random.normal
    f32 = jnp.float32
    P, G, E, F = SSM_STATE, SSM_GROUPS, N_EXPERTS, EXPERT_DIM
    inp = {}
    inp['x'] = nrm(ks[0], (BATCH, SEQ, D_MODEL), f32)
    inp['p'] = nrm(ks[1], (DEPTH, BATCH, SEQ, PLE_DIM), f32)
    inp['g_mix'] = 1.0 + 0.02 * nrm(ks[2], (DEPTH, D_MODEL), f32)
    inp['w_in'] = nrm(ks[3], (DEPTH, D_MODEL, IN_WIDTH), f32) * D_MODEL ** -0.5
    inp['q_norm'] = 1.0 + 0.02 * nrm(ks[4], (DEPTH, HEAD_DIM), f32)
    inp['k_norm'] = 1.0 + 0.02 * nrm(ks[5], (DEPTH, HEAD_DIM), f32)
    inp['w_attn_up'] = nrm(ks[6], (DEPTH, Q_W, D_MODEL), f32) * Q_W ** -0.5
    inp['a_re'] = -0.5 + 0.01 * nrm(ks[7], (DEPTH, N_DIR, G, P), f32)
    inp['a_im'] = math.pi * jnp.arange(P, dtype=f32) + 0.01 * nrm(ks[8], (DEPTH, N_DIR, G, P), f32)
    inp['log_dt'] = jax.random.uniform(ks[9], (DEPTH, N_DIR, G), f32, math.log(1e-3), math.log(1e-1))
    inp['b_re'] = nrm(ks[10], (DEPTH, N_DIR, G, P, SSM_GROUP), f32) * (2 * SSM_GROUP) ** -0.5
    inp['b_im'] = nrm(ks[11], (DEPTH, N_DIR, G, P, SSM_GROUP), f32) * (2 * SSM_GROUP) ** -0.5
    inp['c_re'] = nrm(ks[12], (DEPTH, N_DIR, G, SSM_GROUP, P), f32) * (2 * P) ** -0.5
    inp['c_im'] = nrm(ks[13], (DEPTH, N_DIR, G, SSM_GROUP, P), f32) * (2 * P) ** -0.5
    inp['d_skip'] = nrm(ks[14], (DEPTH, SSM_WIDTH), f32)
    inp['w_glu'] = nrm(ks[15], (DEPTH, SSM_WIDTH, SSM_WIDTH), f32) * SSM_WIDTH ** -0.5
    inp['b_glu'] = 0.01 * nrm(ks[16], (DEPTH, SSM_WIDTH), f32)
    inp['w_ssm_up'] = nrm(ks[17], (DEPTH, SSM_WIDTH, D_MODEL), f32) * SSM_WIDTH ** -0.5
    inp['w_out'] = nrm(ks[18], (DEPTH, D_MODEL, D_MODEL), f32) * D_MODEL ** -0.5
    inp['g_ffn'] = 1.0 + 0.02 * nrm(ks[19], (DEPTH, D_MODEL), f32)
    inp['w_router'] = nrm(ks[20], (DEPTH, D_MODEL, E), f32) * D_MODEL ** -0.5
    inp['router_bias'] = 0.01 * nrm(ks[21], (DEPTH, E), f32)
    inp['w_exp_gate'] = nrm(ks[22], (DEPTH, E, D_MODEL, F), f32) * D_MODEL ** -0.5
    inp['w_exp_up'] = nrm(ks[23], (DEPTH, E, D_MODEL, F), f32) * D_MODEL ** -0.5
    inp['w_exp_down'] = nrm(ks[24], (DEPTH, E, F, D_MODEL), f32) * F ** -0.5
    inp['w_sh_gate'] = nrm(ks[25], (DEPTH, D_MODEL, SHARED_DIM), f32) * D_MODEL ** -0.5
    inp['w_sh_up'] = nrm(ks[26], (DEPTH, D_MODEL, SHARED_DIM), f32) * D_MODEL ** -0.5
    inp['w_sh_down'] = nrm(ks[27], (DEPTH, SHARED_DIM, D_MODEL), f32) * SHARED_DIM ** -0.5
    inp['g_ple'] = 1.0 + 0.02 * nrm(ks[28], (DEPTH, D_MODEL), f32)
    inp['w_ple_gate'] = nrm(ks[29], (DEPTH, D_MODEL, D_MODEL), f32) * D_MODEL ** -0.5
    inp['w_ple_proj'] = nrm(ks[30], (DEPTH, PLE_DIM, D_MODEL), f32) * PLE_DIM ** -0.5
    inp['g_final'] = 1.0 + 0.02 * nrm(ks[31], (D_MODEL,), f32)
    return inp

def reference(x, p, g_mix, w_in, q_norm, k_norm, w_attn_up, a_re, a_im, log_dt, b_re, b_im,
              c_re, c_im, d_skip, w_glu, b_glu, w_ssm_up, w_out, g_ffn, w_router, router_bias,
              w_exp_gate, w_exp_up, w_exp_down, w_sh_gate, w_sh_up, w_sh_down, g_ple,
              w_ple_gate, w_ple_proj, g_final):
    B, L, _ = x.shape
    f32 = jnp.float32
    ROWS = L // GRID_W
    row_ids = jnp.repeat(jnp.arange(ROWS, dtype=f32), GRID_W)
    col_ids = jnp.tile(jnp.arange(GRID_W, dtype=f32), ROWS)
    inv_freq = ROPE_THETA ** (-jnp.arange(0, ROT_HALF, 2, dtype=f32) / ROT_HALF)
    row_ang = row_ids[:, None] * inv_freq[None, :]
    col_ang = col_ids[:, None] * inv_freq[None, :]

    h = x
    for i in range(DEPTH):
        xn = rmsnorm(h, g_mix[i])
        proj = xn @ w_in[i]
        q, k, v, u, gate_a, gate_s = jnp.split(proj, IN_SPLITS, axis=-1)
        q = axial_rope(rmsnorm(q.reshape(B, L, N_HEADS, HEAD_DIM), q_norm[i]), row_ang, col_ang)
        k = axial_rope(rmsnorm(k.reshape(B, L, N_KV_HEADS, HEAD_DIM), k_norm[i]), row_ang, col_ang)
        v = v.reshape(B, L, N_KV_HEADS, HEAD_DIM)
        attn = block_attention(q, k, v)
        ssm = s5_branch(u, a_re[i], a_im[i], log_dt[i], b_re[i], b_im[i], c_re[i], c_im[i],
                        d_skip[i], w_glu[i], b_glu[i])
        merged = (jax.nn.sigmoid(gate_a) * (attn @ w_attn_up[i])
                  + jax.nn.sigmoid(gate_s) * (ssm @ w_ssm_up[i]))
        h = h + merged @ w_out[i]
        h = h + moe(rmsnorm(h, g_ffn[i]), w_router[i], router_bias[i], w_exp_gate[i], w_exp_up[i],
                    w_exp_down[i], w_sh_gate[i], w_sh_up[i], w_sh_down[i])
        ple_gate = jax.nn.sigmoid(rmsnorm(h, g_ple[i]) @ w_ple_gate[i])
        h = h + ple_gate * (p[i] @ w_ple_proj[i])
    return rmsnorm(h, g_final)


_drawn_inputs = setup_inputs


def setup_inputs(seed=0):
    import zlib

    import numpy as np

    out = dict(_drawn_inputs(seed))
    spreads = {}
    factors = {'q_norm': 8.0,
     'k_norm': 4.759,
     'a_re': 8.0,
     'b_glu': 5.101,
     'g_ple': 8.0,
     'g_final': 2.901}
    for name, (base, spread) in spreads.items():
        noise = np.random.default_rng([zlib.crc32(name.encode()), seed]).standard_normal(out[name].shape)
        drawn = base * np.exp(spread * noise) if base else spread * noise
        out[name] = __import__('jax').numpy.asarray(drawn.astype(out[name].dtype))
    for name, factor in factors.items():
        out[name] = (out[name] * factor).astype(out[name].dtype)
    return out
```

```python
from contextlib import ExitStack

import numpy as np

import concourse.bass as bass
from concourse import mybir

F32 = mybir.dt.float32
F32R = mybir.dt.float32r
I32 = mybir.dt.int32
ALU = mybir.AluOpType
ACT = mybir.ActivationFunctionType
AX_X = mybir.AxisListType.X

P = 128
T = 1024
D = 1024
NT = T // P
NC = D // P
HALF = 512
EPS = 1e-6
GRID_W = 64

HEADS, KV, HD = 8, 2, 64
QW, KVW = HEADS * HD, KV * HD
REP = HEADS // KV
SSM = 256
GROUPS, CH, ST = 16, 16, 64
PAIRS = GROUPS // 2
DIRS = 2
DP = DIRS * PAIRS
STEP = 8
NBLK = T // STEP
GATE_A = QW + 2 * KVW + SSM
GATE_S = GATE_A + D

E, F = 64, 128
TOPK, EG, GE, TOPG = 8, 8, 8, 4
SLOTS = P
MAXB = P
AHEAD = 2
SKIP = 4096
RING = 4
SH = 256
PLE = 256
SCALE_ROUTED = 2.5
TWO_PI = 2.0 * np.pi
ROUND = float(3 << 22)

C_ID = 0
C_TRI = C_ID + P
C_COS = C_TRI + P
C_SIN = C_COS + NT * HD
C_TOK = C_SIN + NT * HD
C_COL = C_TOK + NT
C_LOW = C_COL + 1
C_RANK = C_LOW + EG * EG
C_ONE = C_RANK + TOPK
C_END = C_ONE + P


class Order:

    def __init__(self, eng, sem):
        self.eng, self.sem, self.n = eng, sem, 0

    def add(self, ins):
        ins.then_inc(self.sem, 1)
        self.n += 1

    def wait(self):
        self.eng.wait_ge(self.sem, self.n)


def bcast(ap, axis, n):
    a = ap.unsqueeze(axis)
    shape = list(a.shape)
    shape[axis] = n
    return a.to_broadcast(shape)


def build(nc, A, out, dump=None):
    ctx = ExitStack()
    pool = []

    def sb(name, shape, dt=F32):
        cm = nc.sbuf_tensor(name, shape, dt)
        pool.append(cm)
        return cm.__enter__()

    def free_to(n):
        while len(pool) > n:
            pool.pop().__exit__(None, None, None)

    def dram(name, shape, dt=F32):
        return nc.dram_tensor(name, shape, dt, kind="Internal").ap()

    sems = {}

    def S(name):
        if name not in sems:
            sems[name] = ctx.enter_context(nc.semaphore(name))
        return sems[name]

    with ctx:
        psum = ctx.enter_context(nc.psum_tensor("psum", [P, 8, HALF], F32))
        hn_rows = dram("hn_rows", [T, D])
        h1_rows = dram("h1_rows", [T, D])
        h2_rows = dram("h2_rows", [T, D])
        prj_rows = dram("prj_rows", [T, D])
        slot_table = dram("slot_table", [SLOTS * MAXB, 2])

        const = sb("const", [P, C_END])
        ident = const[:, C_ID:C_ID + P]
        ones = const[:, C_ONE:C_ONE + P]
        gcols = sb("gcols", [P, 3, NC])
        stat = sb("stat", [P, 6, NT])
        xnT = sb("xnT", [P, NC, T])
        base = len(pool)

        ssmT = sb("ssmT", [P, 2, T])
        qk = sb("qk", [P, NT, QW + KVW])
        merge_from = len(pool)
        vaug = sb("vaug", [P, NT, KV, 3 * HD])
        rope = sb("rope", [P, 4, NT, HD])
        qkss = sb("qkss", [P, 3, NT, HEADS + KV])
        nrmw = sb("nrmw", [P, 2, HD])
        pool_from = len(pool)

        wqkv = sb("wqkv", [P, NC, QW + 2 * KVW])
        wsu = sb("wsu", [P, DIRS * 2 * PAIRS * P])
        xt = sb("xt", [P, 2, D])
        ublk = sb("ublk", [P, GROUPS, STEP, CH])
        Ug = sb("Ug", [P, GROUPS, NBLK])
        par = sb("par", [P, 3, DP])
        sp = sb("sp", [P, 16, DP])
        bc = sb("bc", [P, 4, DP, CH])
        bb = sb("bb", [P, 2, DP, CH])
        pw = sb("pw", [P, 2, DP, STEP + 1])
        vp = sb("vp", [P, 2, DP, STEP, CH])
        bbz = sb("bbz", [P, 2, PAIRS, 2, CH])
        wy = sb("wy", [P, 2, DP, STEP, CH])
        cblk = sb("cblk", [P, 2, DP, 2, CH])
        dskip = sb("dskip", [P, GROUPS])
        wglu = sb("wglu", [P, 2, SSM])
        bglu = sb("bglu", [P, 2])
        qflat, vflat = qk[:].rearrange("p i n -> p (i n)"), vaug[:].rearrange("p i g n -> p (i g n)")
        xin = [a.rearrange("p (i d) -> p i d", d=D) for a in
               (qflat[:, 0:2 * D], qflat[:, 2 * D:4 * D], xt[:].rearrange("p i d -> p (i d)"), vflat[:, 0:2 * D])]
        tmp = xt
        wu = wsu[:, 0:NC * SSM].rearrange("p (c n) -> p c n", c=NC)
        ws = wsu[:].rearrange("p (d r j m) -> p d r j m", d=DIRS, r=2, j=PAIRS)
        xs = ws
        t0 = ssmT[:].rearrange("p c t -> p (c t)").rearrange("p (g m) -> p g m", g=GROUPS)
        wrot = rope[:].rearrange("p a i d -> p (a i d)").rearrange("p (r j b) -> p r j b", r=2, j=PAIRS)
        resp = rope[:].rearrange("p a i d -> p (a i d)")[:, 0:2 * SSM].rearrange("p (d n) -> p d n", d=2)
        stage = ublk[:].rearrange("p g s c -> p (g s c)").rearrange("p (t n) -> p t n", t=STEP)
        flat = vp[:].rearrange("p r q e c -> p (r q e c)")
        rot = flat.rearrange("p (r q b) -> p r q b", r=2, q=DP)
        yg = ublk[:].rearrange("p g s c -> p g (s c)")
        ytok = Ug[:].rearrange("p g b -> p (g b)").rearrange("p (s c) -> p s c", s=STEP)
        yT = tmp[:]
        sglu = flat[:, 0:2 * T].rearrange("p (r n) -> p r n", r=2)
        qtmp = flat[:, 2 * T:4 * T].rearrange("p (k n) -> p k n", k=2)
        free_to(pool_from)

        qkd = sb("qkd", [P, 2, HEADS + KV, 2, HD])
        QA = sb("QA", [P, HEADS, T], F32R)
        QB = sb("QB", [P, HEADS, T], F32R)
        KA = sb("KA", [P, KV, T], F32R)
        KB = sb("KB", [P, KV, T], F32R)
        pexp = sb("pexp", [P, 3, HALF])
        smax = sb("smax", [P, HEADS, NT])
        smaxT = sb("smaxT", [NT, HEADS, P], F32R)
        rsum = sb("rsum", [P, 2, HALF])
        attnT = qk[:].rearrange("p i n -> p (i n)")[:, 0:4 * T].rearrange("p (c t) -> p c t", c=4)
        free_to(merge_from)

        mergedT = sb("mergedT", [P, NC, T])
        wout = sb("wout", [P, NC, D])
        wmrg = sb("wmrg", [P, 2, 22, P])
        sg = sb("sg", [P, 2, 2, HALF])
        htile = sb("htile", [P, 3, D])
        hntile = sb("hntile", [P, 2, D])
        gffn = sb("gffn", [P, D])
        free_to(base)

        wexp = sb("wexp", [P, RING, NC * 2 * F + D])
        tab = sb("tab", [P, MAXB + AHEAD + 2, 2])
        rows = sb("rows", [P, 2 * P], I32)
        ends = sb("ends", [P, E + 2], I32)
        moe_from = len(pool)
        wrt = sb("wrt", [P, NC, E])
        rbias = sb("rbias", [P, E])
        wsg = sb("wsg", [P, NC, 2, SH])
        wsd = sb("wsd", [P, 2, D])
        shT = sb("shT", [P, 2, T])
        shs = sb("shs", [P, 2, HALF])
        h1t = sb("h1t", [P, 2, D])
        ptok = sb("ptok", [P, 2, PLE])
        pT = sb("pT", [P, 2, T])
        wpp = sb("wpp", [P, 2, D])
        prj = sb("prj", [P, 2, D])
        rt = sb("rt", [P, 12, NT, E])
        oh = sb("oh", [P, 2, TOPK, E])
        grp = sb("grp", [P, 4, NT, EG])
        cmp = sb("cmp", [P, 3, NT, EG * EG])
        dst = sb("dst", [P, 2, NT, TOPK])
        dsti = sb("dsti", [P, NT, TOPK], I32)
        top = sb("top", [P, 2, NT, TOPK])
        blk = sb("blk", [P, 4])
        pay = sb("pay", [P, NT, TOPK, 2])
        cnt = sb("cnt", [P, 6, E])
        free_to(moe_from)
        wpg = sb("wpg", [P, NC, D])
        gfin = sb("gfin", [P, D])
        loop_from = len(pool)
        idx = sb("idx", [P, 4], I32)
        gat = sb("gat", [P, 2])
        xg = sb("xg", [P, 2, D])
        xgT = sb("xgT", [P, 2, NC, P])
        sgm = sb("sgm", [P, 2, F])
        hid = sb("hid", [P, 2, F])
        hidT = sb("hidT", [P, 2, SLOTS])
        yb = sb("yb", [P, 2, D])
        free_to(loop_from)
        h2t = sb("h2t", [P, 3, D])
        ht = sb("ht", [P, 2, D])
        pg = sb("pg", [P, 2, D])
        prjt = sb("prjt", [P, 2, D])
        ot = sb("ot", [P, 2, D])
        hpT = xnT
        free_to(base)
        free_to(0)

        block = ctx.enter_context(nc.Block())

        @block.sync
        def _(sp_):
            dma = sp_.dma_start
            dma(const[:], A["const"]).then_inc(S("ld_const"), 16)
            dma(gcols[:], A["gcols"]).then_inc(S("ld_const"), 16)
            dma(par[:], A["ssm_par"]).then_inc(S("ld_ssm"), 16)
            dma(bc[:], A["ssm_bc"]).then_inc(S("ld_ssm"), 16)
            dma(dskip[:], A["d_skip"]).then_inc(S("ld_ssm"), 16)
            dma(nrmw[:, 0, :], A["q_norm"].partition_broadcast(P)).then_inc(S("ld_norms"), 16)
            dma(nrmw[:, 1, :], A["k_norm"].partition_broadcast(P)).then_inc(S("ld_norms"), 16)
            for i in range(2):
                dma(xin[0][:, i, :], A["x"][P * i:P * i + P]).then_inc(S("ld_x0") if i else S("ld_xfirst"), 16)
            w = A["w_in"].rearrange("(c p) n -> p c n", p=P)
            u0 = QW + 2 * KVW
            for k in range(1, NT // 2):
                dma(xin[k], A["x"][2 * P * k:2 * P * k + 2 * P].rearrange("(i p) d -> p i d", p=P))\
                    .then_inc(S(f"ld_x{k}"), 16)
                if k == 2:
                    dma(wu, w[:, :, u0:GATE_A]).then_inc(S("ld_wu"), 16)
            dma(wqkv[:], w[:, :, 0:u0]).then_inc(S("ld_wqkv"), 16)
            dma(wglu[:], A["w_glu"].rearrange("(k p) n -> p k n", p=P)).then_inc(S("ld_glu"), 16)
            dma(bglu[:], A["b_glu"]).then_inc(S("ld_glu"), 16)
            sp_.wait_ge(S("resp_taken"), 1)
            for t in range(STEP):
                n = CH * (t + 1)
                dma(stage[0:n, t, :], resp[P - n:P, 0, :]).then_inc(S("T0_ready"), 16)
                if n < P:
                    dma(stage[n:P, t, :], resp[CH:CH + P - n, 1, :]).then_inc(S("T0_ready"), 16)
            for h in range(HEADS):
                sp_.wait_ge(S("max_taken"), 9 * h + 9)
                dma(QB[HD:HD + 1, h, :].bitcast(F32), smaxT[:, h, :].bitcast(F32)).then_inc(S(f"mrow{h % 2}"), 16)

            sp_.wait_ge(S("O_taken"), 2 * HEADS)
            w_in = A["w_in"].rearrange("(c p) n -> p c n", p=P)
            w_au = A["w_attn_up"].rearrange("(c p) n -> p c n", p=P)
            w_su = A["w_ssm_up"].rearrange("(c p) n -> p c n", p=P)
            x_tiles = A["x"].rearrange("(i p) d -> i p d", p=P)
            h1_tiles = h1_rows.rearrange("(i p) d -> i p d", p=P)
            hn_tiles = hn_rows.rearrange("(i p) d -> i p d", p=P)
            h2_tiles = h2_rows.rearrange("(i p) d -> i p d", p=P)
            for f_ in range(NC):
                if f_ >= 2:
                    sp_.wait_ge(S("mrg_ready"), 2 * (f_ - 1))
                cols = slice(P * f_, P * f_ + P)
                o = wmrg[:, f_ % 2]
                ld = S(f"ld_m{f_ % 2}")
                dma(o[:, 0:8], w_in[:, :, GATE_A + P * f_:GATE_A + P * f_ + P]).then_inc(ld, 16)
                dma(o[:, 8:16], w_in[:, :, GATE_S + P * f_:GATE_S + P * f_ + P]).then_inc(ld, 16)
                dma(o[:, 16:20], w_au[:, :, cols]).then_inc(ld, 16)
                dma(o[:, 20:22], w_su[:, :, cols]).then_inc(ld, 16)
                if f_ == 1:
                    dma(wout[:], A["w_out"].rearrange("(c p) n -> p c n", p=P)).then_inc(S("ld_out"), 16)
                    dma(gffn[:], A["g_ffn"].partition_broadcast(P)).then_inc(S("ld_out"), 16)
                    for i in range(3):
                        dma(htile[:, i, :], x_tiles[i]).then_inc(S(f"ld_h{i}"), 16)
            for i in range(NT):
                sp_.wait_ge(S("h1_done"), i + 1)
                dma(h1_tiles[i], htile[:, i % 3, :]).then_inc(S("st_h1"), 16)
                sp_.wait_ge(S("hn_done"), i + 1)
                dma(hn_tiles[i], hntile[:, i % 2, :]).then_inc(S("st_hn"), 16)
                sp_.wait_ge(S("st_h1"), 16 * (i + 1))
                sp_.wait_ge(S("st_hn"), 16 * (i + 1))
                sp_.nop().then_inc(S("h_stored"), 1)
                if i + 3 < NT:
                    dma(htile[:, i % 3, :], x_tiles[i + 3]).then_inc(S(f"ld_h{i % 3}"), 16)

            sp_.wait_ge(S("hnT_taken"), 2 * NT)
            dma(wrt[:], A["w_router"].rearrange("(c p) n -> p c n", p=P)).then_inc(S("ld_router"), 16)
            dma(rbias[:], A["router_bias"].partition_broadcast(P)).then_inc(S("ld_router"), 16)
            dma(wpp[:], A["w_ple_proj"].rearrange("(c p) n -> p c n", p=P)).then_inc(S("ld_wpp"), 16)
            p_tiles = A["p"].rearrange("(i p) d -> i p d", p=P)
            prj_tiles = prj_rows.rearrange("(i p) d -> i p d", p=P)
            for i in range(2):
                dma(ptok[:, i, :], p_tiles[i]).then_inc(S(f"ld_p{i}"), 16)
            dma(wsg[:, :, 0, :], A["w_sh_gate"].rearrange("(c p) n -> p c n", p=P)).then_inc(S("ld_wsh"), 16)
            dma(wsg[:, :, 1, :], A["w_sh_up"].rearrange("(c p) n -> p c n", p=P)).then_inc(S("ld_wsh"), 16)
            dma(wsd[:], A["w_sh_down"].rearrange("(c p) n -> p c n", p=P)).then_inc(S("ld_wsh"), 16)
            for e in range(RING):
                dma(wexp[:, e, :], A["w_exp"][e]).then_inc(S(f"ld_w{e}"), 16)
            for i in range(2, NT):
                sp_.wait_ge(S("pT_ready"), i - 1)
                dma(ptok[:, i % 2, :], p_tiles[i]).then_inc(S(f"ld_p{i % 2}"), 16)
            for i in range(NT):
                sp_.wait_ge(S("prj_done"), i + 1)
                dma(prj_tiles[i], prj[:, i % 2, :]).then_inc(S(f"st_prj{i % 2}"), 16)
            for i in range(2):
                dma(h1t[:, i, :], h1_tiles[i]).then_inc(S(f"ld_g{i}"), 16)
            for i in range(NT):
                sp_.wait_ge(S("acc_done"), i + 1)
                dma(h2_tiles[i], h1t[:, i % 2, :]).then_inc(S(f"st_h2{i % 2}"), 16)
                if i + 2 < NT:
                    sp_.wait_ge(S(f"st_h2{i % 2}"), 16 * (i // 2 + 1))
                    dma(h1t[:, i % 2, :], h1_tiles[i + 2]).then_inc(S(f"ld_g{i % 2}"), 16)
            for k in range(2):
                sp_.wait_ge(S(f"st_h2{k}"), 16 * (NT // 2))
            sp_.nop().then_inc(S("h2_stored"), 1)
            dma(wpg[:], A["w_ple_gate"].rearrange("(c p) n -> p c n", p=P)).then_inc(S("ld_last"), 16)
            dma(gfin[:], A["g_final"].partition_broadcast(P)).then_inc(S("ld_last"), 16)

            sp_.wait_ge(S("ends_ready"), 1)
            for e in range(2):
                sp_.wait_ge(S(f"ld_w{e}"), 16)
                sp_.nop().then_inc(S("w_ready"), 1)
            with sp_.Fori(1, E // RING) as q:
                for r in range(RING):
                    last = sp_.value_load(ends[0:1, bass.ds(RING * q + (r - RING), 1)], min_val=0, max_val=MAXB)
                    sp_.wait_ge(S("y_made"), last + 1)
                    dma(wexp[:, r, :], A["w_exp"][bass.ds(RING * q + r, 1)].rearrange("e p n -> p (e n)"))\
                        .then_inc(S(f"ld_w{r}"), 16)
                    k = (r - 2) % RING
                    sp_.wait_ge(S(f"ld_w{k}"), 16 * q + (16 if r >= 2 else 0))
                    sp_.nop().then_inc(S("w_ready"), 1)
            for e in range(E - 2, E):
                sp_.wait_ge(S(f"ld_w{e % RING}"), 16 * (E // RING))
                sp_.nop().then_inc(S("w_ready"), 1)

            sp_.wait_ge(S("moe_done"), 1)
            for i in range(3):
                dma(h2t[:, i, :], h2_tiles[i]).then_inc(S(f"ld_e{i}"), 16)
            for i in range(2):
                dma(prjt[:, i, :], prj_tiles[i]).then_inc(S(f"ld_j{i}"), 16)
            out_tiles = out.rearrange("(i p) d -> i p d", p=P)
            for i in range(NT):
                sp_.wait_ge(S("out_done"), i + 1)
                dma(out_tiles[i], ot[:, i % 2, :]).then_inc(S(f"st_out{i % 2}"), 16)
                if i + 3 < NT:
                    dma(h2t[:, i % 3, :], h2_tiles[i + 3]).then_inc(S(f"ld_e{i % 3}"), 16)
                if i + 2 < NT:
                    dma(prjt[:, i % 2, :], prj_tiles[i + 2]).then_inc(S(f"ld_j{i % 2}"), 16)
            for k in range(2):
                sp_.wait_ge(S(f"st_out{k}"), 16 * (NT // 2))
            if dump:
                sp_.wait_ge(S("O_taken"), 16)
                for name, ap in dump(V()).items():
                    dma(A[name], ap).then_inc(S("dumped"), 16)
                sp_.wait_ge(S("dumped"), 16 * len(dump(V())))

        @block.gpsimd
        def _(pool_):
            nc.gpsimd.memset(bbz[:], 0.0).then_inc(S("tile_set"), 1)
            nc.gpsimd.memset(cblk[:], 0.0).then_inc(S("tile_set"), 1)
            pool_.wait_ge(S("xT_ready"), 2 * NT)
            nc.gpsimd.memset(vaug[:], 1.0).then_inc(S("tile_set"), 1)
            pool_.wait_ge(S("ssm_done"), 1)
            nc.gpsimd.memset(KB[HD:HD + 1].bitcast(F32), 1.0).then_inc(S("KB_ones"), 1)
            pool_.wait_ge(S("KB_ones"), 1)
            for i in range(NT):
                pool_.wait_ge(S("qk_ready"), i + 1)
                if i >= 2:
                    pool_.wait_ge(S("prep_ready"), 3 * (i - 1))
                nc.gpsimd.tensor_copy(qkd[:, i % 2, HEADS:], bcast(qk[:, i, QW:].rearrange("p (h d) -> p h d", d=HD), 2, 2))\
                    .then_inc(S("k_doubled"), 1)

            pool_.wait_ge(S("hnT_taken"), 2 * NT)
            nc.gpsimd.memset(tab[:, :, 0:1], float(SKIP)).then_inc(S("tile_set"), 1)
            nc.gpsimd.memset(tab[:, :, 1:2], 0.0).then_inc(S("tile_set"), 1)
            pool_.wait_ge(S("tile_set"), 5)
            table = slot_table.rearrange("(p b) v -> p (b v)", p=P)
            here = tab[:, 0:MAXB, :].rearrange("p b v -> p (b v)")
            pool_.dma_start(table, here).then_inc(S("table_empty"), 16)
            pool_.wait_ge(S("table_empty"), 16)
            pool_.wait_ge(S("pay_ready"), 1)
            for i in range(NT):
                for k in range(TOPK):
                    pool_.indirect_dma_start(slot_table, bass.IndirectOffsetOnAxis(dsti[:, i, k:k + 1], 0),
                                             pay[:, i, k, :], None).then_inc(S("slots_filled"), 16)
            pool_.wait_ge(S("slots_filled"), 16 * NT * TOPK)
            pool_.dma_start(here, table).then_inc(S("table_read"), 16)
            pool_.wait_ge(S("table_read"), 16)
            pool_.wait_ge(S("h2_stored"), 1)
            nc.gpsimd.memset(xg[:], 0.0).then_inc(S("xg_zero"), 1)
            pool_.wait_ge(S("xg_zero"), 1)


            def gather(t, b):
                nc.gpsimd.tensor_copy(idx[:, b:b + 1], tab[:, bass.ds(t, 1), 0:1].rearrange("p a b -> p (a b)"))\
                    .then_inc(S("gidx"), 1)
                pool_.wait_ge(S("gidx"), t + 1)
                pool_.nop().then_inc(S("pool_turn"), 1)
                pool_.indirect_dma_start(xg[:, b, :], None, hn_rows, bass.IndirectOffsetOnAxis(idx[:, b:b + 1], 0),
                                         bounds_check=T - 1, oob_is_err=False).then_inc(S(f"gathered{b}"), 16)

            def scatter(t, b, early=False):
                nc.gpsimd.tensor_copy(idx[:, 2 + b:3 + b],
                                      tab[:, bass.ds(t, 1), 0:1].rearrange("p a b -> p (a b)"))\
                    .then_inc(S("sidx"), 1)
                pool_.wait_ge(S("sidx"), t + 1)
                pool_.wait_ge(S("ya"), t + 1)
                pool_.wait_ge(S("yd"), t + 1)
                if not early:
                    pool_.wait_ge(S("scattered"), 16 * t)
                pool_.nop().then_inc(S("pool_turn"), 1)
                pool_.indirect_dma_start(h2_rows, bass.IndirectOffsetOnAxis(idx[:, 2 + b:3 + b], 0), yb[:, b, :],
                                         None, bounds_check=T - 1, oob_is_err=False, compute_op=ALU.add)\
                    .then_inc(S("scattered"), 16)

            gather(0, 0)
            gather(1, 1)
            pool_.wait_ge(S("ends_ready"), 1)
            rounds = pool_.value_load(ends[0:1, E + 1:E + 2], min_val=0, max_val=MAXB // 2 - 2)
            pool_.wait_ge(S("xt_ready"), 1)
            gather(2, 0)
            pool_.wait_ge(S("xt_ready"), 2)
            gather(3, 1)
            for k in range(2):
                pool_.wait_ge(S("xt_ready"), 3 + k)
                gather(4 + k, k)
                scatter(k, k, k == 0)
            with pool_.Fori(1, pool_.snap(rounds + 1)) as m:
                for k in range(2):
                    t = 2 * m + (1 + k)
                    pool_.wait_ge(S("xt_ready"), t + 2)
                    gather(t + 3, k)
                    scatter(t - 1, k)
            last = pool_.snap(2 * rounds + 3)
            scatter(last - 1, 0)
            scatter(last, 1)
            pool_.wait_ge(S("gathered0"), 8 * last + 24)
            pool_.wait_ge(S("gathered1"), 8 * last + 24)
            pool_.wait_ge(S("scattered"), 16 * last + 16)
            pool_.nop().then_inc(S("moe_done"), 1)

        @block.scalar
        def _(act):
            own = Order(act, S("act_own"))

            def f(out_, in_, func, **kw):
                return nc.scalar.activation(out_, in_, func, **kw)

            scratch = wy[:].rearrange("p r q s c -> p (r q s c)")
            for i in range(NT):
                act.wait_ge(S(f"ld_x{i // 2}") if i else S("ld_xfirst"), 16)
                own.add(f(scratch[:, 0:D], xin[i // 2][:, i % 2, :], ACT.Square, accum_out=stat[:, 0, i:i + 1]))
                own.wait()
                f(stat[:, 1, i:i + 1], stat[:, 0, i:i + 1], ACT.Sqrt, scale=1.0 / D, bias=EPS)\
                    .then_inc(S("root1"), 1)
            act.wait_ge(S("ld_ssm"), 48)
            f(sp[:, 0, :], par[:, 2, :], ACT.Exp).then_inc(S("dt"), 1)
            act.wait_ge(S("dt_used"), 1)
            f(sp[:, 3, :], sp[:, 1, :], ACT.Exp)
            f(sp[:, 4, :], sp[:, 1, :], ACT.Exp, scale=float(STEP)).then_inc(S("mod"), 1)
            act.wait_ge(S("angles"), 1)
            f(sp[:, 5:9, :], sp[:, 5:9, :], ACT.Sin).then_inc(S("trig"), 1)
            for k in range(STEP):
                act.wait_ge(S("u_ready"), k + 1)
                f(ublk[:, :, k, :], psum[:, 2 + k % 2, 0:SSM].rearrange("p (g c) -> p g c", c=CH), ACT.Copy).then_inc(S("u_taken"), 1)
            for q in range(4):
                act.wait_ge(S("Ut_ready"), q + 1)
                f(Ug[:, 4 * q:4 * q + 4, :], psum[:, 4 + q % 2, :], ACT.Copy).then_inc(S("Ug_taken"), 1)
            def take_qkv(i):
                b = 2 * (i % 2)
                act.wait_ge(S("qkv_ready"), i + 1)
                f(qk[:, i, 0:QW], psum[:, b, :], ACT.Copy)
                f(qk[:, i, QW:QW + KVW], psum[:, b + 1, 0:KVW], ACT.Copy)
                v_ = psum[:, b + 1, KVW:2 * KVW].rearrange("p (g d) -> p g d", g=KV)
                f(vaug[:, i, :, 0:HD], v_, ACT.Copy)
                f(vaug[:, i, :, 2 * HD:3 * HD], v_, ACT.Copy).then_inc(S("qkv_taken"), 1)

            def root_qk(half):
                ts = slice(NT // 2 * half, NT // 2 * half + NT // 2)
                act.wait_ge(S("qkss_ready"), half + 1)
                f(qkss[:, 1, ts], qkss[:, 0, ts], ACT.Sqrt, scale=1.0 / HD, bias=EPS).then_inc(S("qkroot"), 1)

            act.wait_ge(S("tile_set"), 3)
            take_qkv(0)
            take_qkv(1)
            act.wait_ge(S("resp_ready"), 1)
            f(resp, psum[:, 4:6, 0:SSM], ACT.Copy).then_inc(S("resp_taken"), 1)
            for k in range(8):
                d, r, q = k // 4, k // 2 % 2, k % 2
                act.wait_ge(S("ws_ready"), k + 1)
                f(ws[:, d, r, 4 * q:4 * q + 4, :], psum[:, 6 + k % 2, :], ACT.Copy).then_inc(S("ws_taken"), 1)
            for i in range(2, NT):
                take_qkv(i)
                if i == NT - 2:
                    root_qk(0)
            root_qk(1)
            for q in range(4):
                act.wait_ge(S("y_ready"), q + 1)
                b = 2 * (q % 2)
                f(yg[:, 4 * q:4 * q + 4, :].rearrange("p (k h) b -> p h k b", h=2),
                  psum[:, b:b + 2, 0:2 * NBLK].rearrange("p h (k b) -> p h k b", k=2), ACT.Gelu_apprx_tanh)\
                    .then_inc(S("y_taken"), 1)
            for q in range(4):
                act.wait_ge(S("yk_ready"), q + 1)
                o = ytok.rearrange("p s (g c) -> p g s c", c=CH)[:, 4 * q:4 * q + 4]
                i_ = psum[:, 2 + q % 2, :].rearrange("p (g s c) -> p g s c", g=4, s=STEP)
                f(o, i_, ACT.Copy).then_inc(S("yk_taken"), 1)
            for k in range(4):
                hh, q = k // 2, k % 2
                act.wait_ge(S("yT_ready"), k + 1)
                o = yT[:, hh, :].rearrange("p (b s) -> p s b", s=STEP)[:, 4 * q:4 * q + 4, :]
                i_ = psum[:, 4 + k, :].rearrange("p (s b) -> p s b", s=4)
                f(o, i_, ACT.Copy).then_inc(S("yT_taken"), 1)
            act.wait_ge(S("ld_glu"), 32)
            for k in range(4):
                co, th = k // 2, k % 2
                act.wait_ge(S("glu_ready"), k + 1)
                f(sglu[:, co, HALF * th:HALF * th + HALF], psum[:, k, :], ACT.Sigmoid, bias=bglu[:, co:co + 1])\
                    .then_inc(S("glu_sig"), 1)
            act.wait_ge(S("ssm_done"), 1)
            for n in range(3 * NT):
                i, part = n // 3, n % 3
                tok = slice(P * i, P * i + P)
                act.wait_ge(S("prep_ready"), n + 1)
                src = psum[:, n % 4, :].rearrange("p (h t) -> p h t", t=P)
                if part < 2:
                    f(QA[:, 4 * part:4 * part + 4, tok], src, ACT.Copy).then_inc(S("hi_done"), 1)
                else:
                    f(KB[0:HD, :, tok], src[0:HD, 0:KV, :], ACT.Copy)
                    f(KA[:, :, tok], src[:, 0:KV, :], ACT.Copy).then_inc(S("hi_done"), 1)
            for n in range(HEADS * 2 * NT):
                act.wait_ge(S("sT_ready"), n + 1)
                if n >= 3:
                    act.wait_ge(S("pv_done"), n - 2)
                f(pexp[:, n % 3, :], psum[:, 4 + n % 2, :], ACT.Exp).then_inc(S("exp_done"), 1)

            act.wait_ge(S("O_taken"), 2 * HEADS)
            for n in range(2 * NC):
                b = 4 * (n % 2)
                act.wait_ge(S("mrg_ready"), n + 1)
                if n >= 2:
                    act.wait_ge(S("mrg_taken"), n - 1)
                f(sg[:, n % 2, 0, :], psum[:, b, :], ACT.Sigmoid)
                f(sg[:, n % 2, 1, :], psum[:, b + 2, :], ACT.Sigmoid).then_inc(S("sg_done"), 1)
            act.wait_ge(S("mrg_taken"), 2 * NC)
            scratch = sg[:].rearrange("p a b n -> p (a b n)")
            for i in range(NT + 1):
                if i < NT:
                    act.wait_ge(S("h1_done"), i + 1)
                    own.wait()
                    own.add(f(scratch[:, 0:D], htile[:, i % 3, :], ACT.Square, accum_out=stat[:, 3, i:i + 1]))
                    own.wait()
                    f(stat[:, 4, i:i + 1], stat[:, 3, i:i + 1], ACT.Sqrt, scale=1.0 / D, bias=EPS)\
                        .then_inc(S("root2"), 1)
                if i >= 1:
                    for j in range(2):
                        n = 2 * (i - 1) + j
                        act.wait_ge(S("hnT_ready"), n + 1)
                        f(xnT[:, 4 * j:4 * j + 4, P * (i - 1):P * i],
                          psum[:, 4 + n % 4, :].rearrange("p (c t) -> p c t", c=4), ACT.Copy)\
                            .then_inc(S("hnT_taken"), 1)
            act.wait_ge(S("lg_ready"), 1)
            act.wait_ge(S("hnT_taken"), 2 * NT)
            act.wait_ge(S("h_stored"), NT)
            f(rt[:, 0].rearrange("p i e -> p (i e)"), psum[:, 0, :], ACT.Sigmoid).then_inc(S("sc_done"), 1)
            for i in range(NT):
                act.wait_ge(S("pT_ready"), i + 1)
                f(pT[:, :, P * i:P * i + P], psum[:, 1 + i % 2, 0:2 * P].rearrange("p (c t) -> p c t", c=2),
                  ACT.Copy).then_inc(S("pT_taken"), 1)
            for i in range(NT):
                b = 4 + 2 * (i % 2)
                act.wait_ge(S("prj_ready"), i + 1)
                if i >= 2:
                    act.wait_ge(S(f"st_prj{i % 2}"), 16 * (i // 2))
                f(prj[:, i % 2, :], psum[:, b:b + 2, :].rearrange("p k n -> p (k n)"), ACT.Copy)\
                    .then_inc(S("prj_done"), 1)
            for n in range(4):
                act.wait_ge(S("shgu_ready"), n + 1)
                if n >= 2:
                    act.wait_ge(S("sh_taken"), n - 1)
                f(shs[:, n % 2, :], psum[:, 4 + 2 * (n % 2), :], ACT.Silu).then_inc(S("shs_done"), 1)

            act.wait_ge(S("ends_ready"), 1)
            act.wait_ge(S("h2_stored"), 1)
            rounds = act.value_load(ends[0:1, E + 1:E + 2], min_val=0, max_val=MAXB // 2 - 2)

            def take_x(t, b, early=False):
                act.wait_ge(S("xt_ready"), t + 1)
                if not early:
                    act.wait_ge(S("gu_ready"), t - 1)
                f(xgT[:, b, 0:4, :].rearrange("p c s -> p (c s)"), psum[:, 0, :], ACT.Copy).then_inc(S("xa"), 1)

            def silu(t, b, early=False):
                act.wait_ge(S("gu_ready"), t + 1)
                if not early:
                    act.wait_ge(S("hid_ready"), t - 1)
                f(sgm[:, b, :], psum[:, 2 + b, 0:F], ACT.Silu).then_inc(S("sgm_ready"), 1)

            def take_y(t, b, early=False):
                act.wait_ge(S("y_made"), t + 2)
                if not early:
                    act.wait_ge(S("scattered"), 16 * t - 16)
                f(yb[:, b, 0:HALF], psum[:, 5, :], ACT.Copy, scale=tab[:, bass.ds(t, 1), 1:2].rearrange(
                    "p a b -> p (a b)")).then_inc(S("ya"), 1)

            act.wait_ge(S("table_read"), 16)
            take_x(0, 0, True)
            take_x(1, 1, True)
            silu(0, 0, True)
            for k in range(2):
                t = 1 + k
                take_x(t + 1, k % 2, False)
                silu(t, (1 + k) % 2, t < 2)
                take_y(t - 1, k, True)
            with act.Fori(1, act.snap(rounds + 1)) as m:
                for k in range(2):
                    t = 2 * m + (1 + k)
                    take_x(t + 1, k)
                    silu(t, (1 + k) % 2)
                    take_y(t - 1, k)
            last = act.snap(2 * rounds + 3)
            silu(last, 1)
            take_y(last - 1, 0)
            take_y(last, 1)

            act.wait_ge(S("moe_done"), 1)
            scratch = ht[:, 0, :]

            def gate_of(i):
                b = 4 + 2 * (i % 2)
                act.wait_ge(S("pg_ready"), i + 1)
                if i >= 2:
                    act.wait_ge(S("out_done"), i - 1)
                f(pg[:, i % 2, :], psum[:, b:b + 2, :].rearrange("p k n -> p (k n)"), ACT.Sigmoid)\
                    .then_inc(S("pg_done"), 1)

            def norm_of(i):
                act.wait_ge(S("h3_done"), i + 1)
                own.add(f(ot[:, i % 2, :], pg[:, i % 2, :], ACT.Square, accum_out=stat[:, 3, i:i + 1]))
                own.wait()
                f(stat[:, 4, i:i + 1], stat[:, 3, i:i + 1], ACT.Sqrt, scale=1.0 / D, bias=EPS)\
                    .then_inc(S("root4"), 1)

            for i in range(NT + 2):
                if i < NT:
                    act.wait_ge(S(f"ld_e{i % 3}"), 16 * (i // 3 + 1))
                    if i >= 2:
                        act.wait_ge(S("ht_ready"), 2 * (i - 1))
                    own.add(f(ht[:, i % 2, :], h2t[:, i % 3, :], ACT.Square, accum_out=stat[:, 0, i:i + 1]))
                    own.wait()
                    f(stat[:, 1, i:i + 1], stat[:, 0, i:i + 1], ACT.Sqrt, scale=1.0 / D, bias=EPS)\
                        .then_inc(S("root3"), 1)
                if i >= 2:
                    if i >= 4:
                        act.wait_ge(S(f"st_out{i % 2}"), 16 * (i // 2 - 1))
                    gate_of(i - 2)
                    norm_of(i - 2)

        @block.vector
        def _(dve):
            own = Order(dve, S("dve_own"))
            v = nc.vector

            def tt(o, a, b, op):
                own.add(v.tensor_tensor(o, a, b, op))

            def tsc(o, a, s1, op0, s2=None, op1=None):
                own.add(v.tensor_scalar(o, a, s1, s2, op0, op1) if op1 is not None
                        else v.tensor_scalar(o, a, s1, None, op0))

            def cmul(o, a, b, t, neg_im=False):
                tt(o[0], a[0], b[0], ALU.mult)
                tt(t[0], a[1], b[1], ALU.mult)
                tt(o[1], a[0], b[1], ALU.mult)
                tt(t[1], a[1], b[0], ALU.mult)
                own.wait()
                tt(o[0], o[0], t[0], ALU.subtract)
                if neg_im:
                    own.add(v.scalar_tensor_tensor(out=o[1], in0=o[1], scalar=-1.0, in1=t[1],
                                                   op0=ALU.mult, op1=ALU.subtract))
                else:
                    tt(o[1], o[1], t[1], ALU.add)
                own.wait()

            dve.wait_ge(S("ld_const"), 32)

            def evac_x(i):
                for j in range(2):
                    dve.wait_ge(S("xT_ready"), 2 * i + j + 1)
                    v.tensor_tensor(xnT[:, 4 * j:4 * j + 4, P * i:P * i + P],
                                    psum[:, j, :].rearrange("p (c t) -> p c t", c=4),
                                    bcast(gcols[:, 0, 4 * j:4 * j + 4], 2, P), ALU.mult)\
                        .then_inc(S("xT_taken"), 1)

            for i in range(NT):
                dve.wait_ge(S("root1"), i + 1)
                own.add(v.reciprocal(stat[:, 2, i:i + 1], stat[:, 1, i:i + 1]))
                own.wait()
                v.tensor_scalar(xin[i // 2][:, i % 2, :], xin[i // 2][:, i % 2, :], stat[:, 2, i:i + 1], None, ALU.mult)\
                    .then_inc(S("xs_ready"), 1)
                if i >= 1:
                    evac_x(i - 1)
            evac_x(NT - 1)

            t4 = [tmp[:, k, :] for k in range(2)]
            DT, LR, LI, ER, R8, S1, S8, C1, C8, FR, FI, T1, T2, T3, T4 = range(15)

            def c_(k):
                return sp[:, k, :]

            dve.wait_ge(S("dt"), 1)
            tt(c_(LR), par[:, 0, :], c_(DT), ALU.mult)
            tt(c_(LI), par[:, 1, :], c_(DT), ALU.mult)
            own.wait()
            v.engine_nop().then_inc(S("dt_used"), 1)
            tsc(c_(S1), c_(LI), 1.0, ALU.mult)
            tsc(c_(S8), c_(LI), float(STEP), ALU.mult)
            own.wait()
            ang = sp[:, S1:S8 + 1, :]
            turns = sp[:, T1:T2 + 1, :]
            tsc(turns, ang, 1.0 / TWO_PI, ALU.mult, ROUND, ALU.add)
            own.wait()
            tsc(turns, turns, ROUND, ALU.subtract)
            own.wait()
            part, rest = [], TWO_PI
            for bits in (8, 16):
                part.append(float(np.round(rest * 2.0 ** bits) / 2.0 ** bits))
                rest -= part[-1]
            for piece in part + [float(np.float32(rest))]:
                own.add(v.scalar_tensor_tensor(out=ang, in0=turns, scalar=-piece, in1=ang,
                                               op0=ALU.mult, op1=ALU.add))
                own.wait()
            tsc(ang, ang, float(np.pi), ALU.min, -float(np.pi), ALU.max)
            own.wait()
            cosa = sp[:, C1:C8 + 1, :]
            own.add(v.scalar_tensor_tensor(out=cosa, in0=ang, scalar=-1.0, in1=ang, op0=ALU.mult, op1=ALU.max))
            own.wait()
            tsc(cosa, cosa, -1.0, ALU.mult, float(np.pi / 2), ALU.add)
            own.wait()
            v.engine_nop().then_inc(S("angles"), 1)
            dve.wait_ge(S("mod"), 1)
            dve.wait_ge(S("trig"), 1)
            own.add(v.memset(pw[:, 0, :, 0:1], 1.0))
            own.add(v.memset(pw[:, 1, :, 0:1], 0.0))
            tt(pw[:, 0, :, 1], c_(ER), c_(C1), ALU.mult)
            tt(pw[:, 1, :, 1], c_(ER), c_(S1), ALU.mult)
            own.wait()
            for lo, n, by in ((1, 1, 1), (1, 2, 2), (1, 4, 4)):
                cmul([pw[:, r, :, by + lo:by + lo + n] for r in range(2)],
                     [pw[:, r, :, lo:lo + n] for r in range(2)],
                     [pw[:, r, :, by:by + 1].to_broadcast([P, DP, n]) for r in range(2)],
                     [t4[k][:, 0:DP * n].rearrange("p (q n) -> p q n", n=n) for k in range(2)])
            tsc(c_(T3), pw[:, 0, :, 1], 1.0, ALU.subtract)
            tt(c_(T1), par[:, 0, :], par[:, 0, :], ALU.mult)
            tt(c_(T2), par[:, 1, :], par[:, 1, :], ALU.mult)
            own.wait()
            tt(c_(T1), c_(T1), c_(T2), ALU.add)
            own.wait()
            own.add(v.reciprocal(c_(T1), c_(T1)))
            tt(c_(FR), c_(T3), par[:, 0, :], ALU.mult)
            tt(c_(T2), pw[:, 1, :, 1], par[:, 1, :], ALU.mult)
            tt(c_(FI), pw[:, 1, :, 1], par[:, 0, :], ALU.mult)
            tt(c_(T4), c_(T3), par[:, 1, :], ALU.mult)
            own.wait()
            tt(c_(FR), c_(FR), c_(T2), ALU.add)
            tt(c_(FI), c_(FI), c_(T4), ALU.subtract)
            own.wait()
            tt(c_(FR), c_(FR), c_(T1), ALU.mult)
            tt(c_(FI), c_(FI), c_(T1), ALU.mult)
            own.wait()
            dve.wait_ge(S("ld_ssm"), 48)
            dve.wait_ge(S("tile_set"), 2)
            cmul([bb[:, 0], bb[:, 1]], [bc[:, 0], bc[:, 1]],
                 [bcast(c_(FR), 2, CH), bcast(c_(FI), 2, CH)],
                 [t4[k][:, 0:DP * CH].rearrange("p (q c) -> p q c", c=CH) for k in range(2)])
            shaped = [t4[k].rearrange("p (q s c) -> p q s c", s=STEP, c=CH) for k in range(2)]
            for d in range(DIRS):
                q = slice(PAIRS * d, PAIRS * d + PAIRS)
                powers = pw[:, :, q, STEP - 1::-1] if d == 0 else pw[:, :, q, 0:STEP]
                cmul([vp[:, r, q] for r in range(2)],
                     [bcast(bb[:, r, q, :], 2, STEP) for r in range(2)],
                     [bcast(powers[:, r], 3, CH) for r in range(2)], shaped)
            for gg in range(2):
                rows_ = slice(ST * gg, ST * gg + ST)
                own.add(v.tensor_copy(cblk[rows_, 0, :, gg, :], bc[rows_, 2]))
                tsc(cblk[rows_, 1, :, gg, :], bc[rows_, 3], -1.0, ALU.mult)
            own.add(v.tensor_copy(bbz[:, :, :, 1, :], bb[:, :, PAIRS:DP, :]))
            own.wait()
            v.engine_nop().then_inc(S("vp_ready"), 1)
            for d in range(DIRS):
                q = slice(PAIRS * d, PAIRS * d + PAIRS)
                powers = pw[:, :, q, 1:STEP + 1] if d == 0 else pw[:, :, q, STEP:0:-1]
                cmul([wy[:, r, q] for r in range(2)],
                     [bcast(bc[:, 2 + r, q, :], 2, STEP) for r in range(2)],
                     [bcast(powers[:, r], 3, CH) for r in range(2)], shaped, neg_im=True)

            dve.wait_ge(S("ws_ready"), 8)
            own.add(v.memset(rot[:, 0, :, 0:1], 1.0))
            own.add(v.memset(rot[:, 1, :, 0:1], 0.0))
            own.add(v.tensor_copy(rot[:, 0, :, 1], c_(C8)))
            own.add(v.tensor_copy(rot[:, 1, :, 1], c_(S8)))
            own.wait()
            n = 2
            while n < NBLK:
                cmul([c_(T3), c_(T4)], [rot[:, r, :, n // 2] for r in range(2)],
                     [rot[:, r, :, n // 2] for r in range(2)], [c_(T1), c_(T2)])
                cmul([rot[:, r, :, n:2 * n] for r in range(2)], [rot[:, r, :, 0:n] for r in range(2)],
                     [bcast(c_(T3), 2, n), bcast(c_(T4), 2, n)],
                     [t4[k][:, 0:DP * n].rearrange("p (q n) -> p q n", n=n) for k in range(2)])
                n *= 2
            dve.wait_ge(S("ld_ssm"), 48)
            dve.wait_ge(S("T0_ready"), 16 * (2 * STEP - 1))
            for g in range(GROUPS):
                own.add(v.scalar_tensor_tensor(out=t0[:, g, :].rearrange("p (t c) -> p t c", t=STEP),
                                               in0=ident.rearrange("p (t c) -> p t c", t=STEP),
                                               scalar=dskip[:, g:g + 1], in1=stage[:, :, CH * g:CH * g + CH],
                                               op0=ALU.mult, op1=ALU.add))
            own.wait()
            v.engine_nop().then_inc(S("T0_taken"), 1)
            for d in range(DIRS):
                dve.wait_ge(S("S_ready"), d + 1)
                co, si = (rot[:, r, PAIRS * d:PAIRS * d + PAIRS, :] for r in range(2))
                sre = psum[:, 4:6, :].rearrange("p k (j b) -> p (k j) b", b=NBLK)
                sim = psum[:, 6:8, :].rearrange("p k (j b) -> p (k j) b", b=NBLK)
                wre, wim = wrot[:, 0], wrot[:, 1]
                ta, tb = (t4[k].rearrange("p (j b) -> p j b", b=NBLK) for k in range(2))
                tt(wre, co, sre, ALU.mult)
                tt(ta, si, sim, ALU.mult)
                tt(wim, co, sim, ALU.mult)
                tt(tb, si, sre, ALU.mult)
                own.wait()
                v.engine_nop().then_inc(S("S_taken"), 1)
                tt(wre, wre, ta, ALU.add)
                tt(wim, wim, tb, ALU.subtract)
                own.wait()
                for r in range(2):
                    for j in range(PAIRS):
                        decay = sp[:, R8, PAIRS * d + j:PAIRS * d + j + 1].to_broadcast([P, NBLK])
                        own.add(v.tensor_tensor_scan(wrot[:, r, j, :], decay, wrot[:, r, j, :], 0.0,
                                                     ALU.mult, ALU.add))
                own.wait()
                keep = slice(0, NBLK - 1)
                xre, xim = (xs[:, d, r, :, 1:NBLK] for r in range(2))
                for r in range(2):
                    own.add(v.memset(xs[:, d, r, :, 0:1], 0.0))
                tt(xre, co[:, :, keep], wre[:, :, keep], ALU.mult)
                tt(ta[:, :, keep], si[:, :, keep], wim[:, :, keep], ALU.mult)
                tt(xim, co[:, :, keep], wim[:, :, keep], ALU.mult)
                tt(tb[:, :, keep], si[:, :, keep], wre[:, :, keep], ALU.mult)
                own.wait()
                tt(xre, xre, ta[:, :, keep], ALU.subtract)
                tt(xim, xim, tb[:, :, keep], ALU.add)
                own.wait()
                v.engine_nop().then_inc(S("X_ready"), 1)
            def heads(ap):
                return ap.rearrange("p (h d) -> p h d", d=HD)

            dve.wait_ge(S("ld_norms"), 32)
            cos_ = const[:, C_COS:C_COS + NT * HD].rearrange("p (i d) -> p i d", i=NT)
            sin_ = const[:, C_SIN:C_SIN + NT * HD].rearrange("p (i d) -> p i d", i=NT)
            for m in range(2):
                scale = HD ** -0.5 if m == 0 else 1.0
                w = nrmw[:, m, :]
                tt(rope[:, 2 * m], cos_, bcast(w, 1, NT), ALU.mult)
                for s_ in range(2):
                    o = rope[:, 2 * m + 1].rearrange("p i (a s f) -> p i a s f", a=2, s=2)[:, :, :, s_]
                    i0 = sin_.rearrange("p i (a s f) -> p i a s f", a=2, s=2)[:, :, :, s_]
                    i1 = w.rearrange("p (a s f) -> p a s f", a=2, s=2)[:, :, 1 - s_]
                    tt(o, i0, bcast(i1, 1, NT), ALU.mult)
                own.wait()
                if m == 0:
                    tsc(rope[:, 0], rope[:, 0], scale, ALU.mult)
                    tsc(rope[:, 1], rope[:, 1], scale, ALU.mult)
            for half in range(2):
                ts = slice(NT // 2 * half, NT // 2 * half + NT // 2)
                if half:
                    dve.wait_ge(S("qk_ready"), NT // 2)
                for i in range(NT // 2 * half, NT // 2 * half + NT // 2):
                    dve.wait_ge(S("qkv_taken"), i + 1)
                    tt(qtmp[:, i % 2, 0:QW + KVW], qk[:, i], qk[:, i], ALU.mult)
                    own.wait()
                    own.add(v.tensor_reduce(qkss[:, 0, i, :], heads(qtmp[:, i % 2, 0:QW + KVW]), AX_X, ALU.add))
                own.wait()
                v.engine_nop().then_inc(S("qkss_ready"), 1)
                dve.wait_ge(S("qkroot"), half + 1)
                own.add(v.reciprocal(qkss[:, 2, ts], qkss[:, 1, ts]))
                own.wait()
                for i in range(NT // 2 * half, NT // 2 * half + NT // 2):
                    if i >= 1:
                        dve.wait_ge(S("qk_ready"), i)
                    for m, (at, n) in enumerate(((0, HEADS), (QW, KV))):
                        src = qk[:, i, at:at + n * HD]
                        t1 = qtmp[:, 0, at:at + n * HD]
                        t2 = qtmp[:, 1, at:at + n * HD]
                        tt(heads(t1), heads(src), bcast(rope[:, 2 * m, i], 1, n), ALU.mult)
                        for s_ in range(2):
                            def part(ap, k):
                                return ap.rearrange("p (h a s f) -> p h a s f", a=2, s=2, f=HD // 4)[:, :, :, k]
                            sn = rope[:, 2 * m + 1, i].rearrange("p (a s f) -> p a s f", a=2, s=2)[:, :, s_]
                            tt(part(t2, s_), part(src, 1 - s_), bcast(sn, 1, n), ALU.mult)
                    own.wait()
                    both = qtmp[:, 0, 0:QW + KVW]
                    tt(both, both, qtmp[:, 1, 0:QW + KVW], ALU.add)
                    own.wait()
                    v.tensor_tensor(heads(qk[:, i]), heads(both), bcast(qkss[:, 2, i], 2, HD), ALU.mult)\
                        .then_inc(S("qk_ready"), 1)

            for k in range(4):
                co_, th = k // 2, k % 2
                cols = slice(HALF * th, HALF * th + HALF)
                dve.wait_ge(S("glu_sig"), k + 1)
                tt(ssmT[:, co_, cols], yT[:, co_, cols], sglu[:, co_, cols], ALU.mult)
            own.wait()
            v.engine_nop().then_inc(S("ssm_done"), 1)

            for n in range(3 * NT):
                i, part = n // 3, n % 3
                if part == 0:
                    for j in [0, 1] if i == 0 else [i + 1] if i + 1 < NT else []:
                        if j >= 2:
                            dve.wait_ge(S("prep_ready"), 3 * (j - 1) - 1)
                        v.tensor_copy(qkd[:, j % 2, 0:HEADS], bcast(heads(qk[:, j, 0:QW]), 2, 2))\
                            .then_inc(S("q_doubled"), 1)
                tok = slice(P * i, P * i + P)
                dve.wait_ge(S("hi_done"), n + 1)
                src = psum[:, n % 4, :].rearrange("p (h t) -> p h t", t=P)
                if part < 2:
                    hs = slice(4 * part, 4 * part + 4)
                    ins = v.tensor_tensor(QB[0:HD, hs, tok], src[0:HD], QA[0:HD, hs, tok].bitcast(F32),
                                          ALU.subtract)
                else:
                    ins = v.tensor_tensor(KA[HD:P, :, tok], src[HD:P, 0:KV, :], KA[HD:P, :, tok].bitcast(F32),
                                          ALU.subtract)
                ins.then_inc(S("prep_taken"), 1)

            def row_max(h, i):
                m = 9 * h + i
                dve.wait_ge(S("max_ready"), m + 1)
                b = 2 * (m % 2)
                if i < NT:
                    v.tensor_reduce(smax[:, h, i:i + 1], psum[:, b:b + 2, :].rearrange("p k n -> p (k n)"),
                                    AX_X, ALU.max).then_inc(S("max_taken"), 1)
                else:
                    v.tensor_scalar(smaxT[:, h, :], psum[0:NT, b, 0:P], -1.0, None, ALU.mult)\
                        .then_inc(S("max_taken"), 1)

            def finish_head(h, qh):
                n = 2 * h + qh
                dve.wait_ge(S("pv_done"), NT * (n + 1))
                a0, s0 = (0, HD) if h % 2 == 0 else (HD, 0)
                b = 6 + n % 2
                own.add(v.reciprocal(rsum[a0:a0 + HD, qh, :], psum[s0:s0 + HD, b, :]))
                own.wait()
                v.tensor_tensor(attnT[a0:a0 + HD, h // 2, HALF * qh:HALF * qh + HALF], psum[a0:a0 + HD, b, :],
                                rsum[a0:a0 + HD, qh, :], ALU.mult).then_inc(S("O_taken"), 1)

            for h in range(2):
                for i in range(NT + 1):
                    row_max(h, i)
            for h in range(HEADS):
                for k in range(2 * NT):
                    if k == 1 and h >= 1:
                        finish_head(h - 1, 1)
                    if k == NT + 1:
                        finish_head(h, 0)
                    if k % 2 == 1 and h + 2 < HEADS:
                        row_max(h + 2, k // 2)
                if h + 2 < HEADS:
                    row_max(h + 2, NT)
            finish_head(HEADS - 1, 1)

            for n in range(2 * NC):
                b = 4 * (n % 2)
                s0, s1 = sg[:, n % 2, 0, :], sg[:, n % 2, 1, :]
                dve.wait_ge(S("sg_done"), n + 1)
                tt(s0, s0, psum[:, b + 1, :], ALU.mult)
                tt(s1, s1, psum[:, b + 3, :], ALU.mult)
                own.wait()
                v.tensor_tensor(mergedT[:, n // 2, HALF * (n % 2):HALF * (n % 2) + HALF], s0, s1, ALU.add)\
                    .then_inc(S("mrg_taken"), 1)
            dve.wait_ge(S("ld_out"), 32)
            for i in range(NT + 1):
                if i < NT:
                    b = 2 * (i % 2)
                    h = htile[:, i % 3, :]
                    dve.wait_ge(S(f"ld_h{i % 3}"), 16 * (i // 3 + 1))
                    dve.wait_ge(S("wo_ready"), i + 1)
                    v.tensor_tensor(h, h, psum[:, b:b + 2, :].rearrange("p k n -> p (k n)"), ALU.add)\
                        .then_inc(S("h1_done"), 1)
                if i >= 1:
                    k = i - 1
                    dve.wait_ge(S("root2"), k + 1)
                    own.add(v.reciprocal(stat[:, 5, k:k + 1], stat[:, 4, k:k + 1]))
                    own.wait()
                    if k >= 2:
                        dve.wait_ge(S("h_stored"), k - 1)
                        dve.wait_ge(S("hnT_ready"), 2 * (k - 1))
                    v.scalar_tensor_tensor(out=hntile[:, k % 2, :], in0=htile[:, k % 3, :],
                                           scalar=stat[:, 5, k:k + 1], in1=gffn[:], op0=ALU.mult,
                                           op1=ALU.mult).then_inc(S("hn_done"), 1)

            dve.wait_ge(S("sc_done"), 1)
            dve.wait_ge(S("ld_router"), 32)
            SC, BIASED, MASKED, REPLACED, SEL, GATE, BEFORE, DIV, DEST, CUM, RANK = range(11)

            def r_(k):
                return rt[:, k]

            def byg(k):
                return rt[:, k].rearrange("p i (g e) -> p i g e", g=EG)

            tt(r_(BIASED), r_(SC), bcast(rbias[:], 1, NT), ALU.add)
            own.wait()
            best = cmp[:, 0].rearrange("p i (g k) -> p i g k", g=EG)
            for i in range(NT):
                for g in range(EG):
                    own.add(v.max(best[:, i, g, :], rt[:, BIASED, i, GE * g:GE * g + GE]))
            own.wait()
            tt(grp[:, 0], best[:, :, :, 0], best[:, :, :, 1], ALU.add)
            own.wait()
            mine = bcast(grp[:, 0], 3, EG)
            other = bcast(grp[:, 0], 2, EG)
            gt, eq = (cmp[:, k].rearrange("p i (g h) -> p i g h", g=EG) for k in (1, 2))
            tt(gt, other, mine, ALU.is_gt)
            tt(eq, other, mine, ALU.is_equal)
            own.wait()
            tt(cmp[:, 2], cmp[:, 2], bcast(const[:, C_LOW:C_LOW + EG * EG], 1, NT), ALU.mult)
            own.wait()
            tt(cmp[:, 1], cmp[:, 1], cmp[:, 2], ALU.add)
            own.wait()
            own.add(v.tensor_reduce(grp[:, 1], gt, AX_X, ALU.add))
            own.wait()
            tsc(grp[:, 2], grp[:, 1], float(TOPG), ALU.is_lt)
            own.wait()
            tsc(grp[:, 3], grp[:, 2], 1.0, ALU.subtract, 1e30, ALU.mult)
            tt(byg(MASKED), byg(BIASED), bcast(grp[:, 2], 3, GE), ALU.mult)
            own.wait()
            tt(byg(MASKED), byg(MASKED), bcast(grp[:, 3], 3, GE), ALU.add)
            own.wait()
            for i in range(NT):
                own.add(v.max(top[:, 0, i, :], rt[:, MASKED, i, :]))
            own.wait()
            for i in range(NT):
                own.add(v.match_replace(rt[:, REPLACED, i, :], top[:, 0, i, :], rt[:, MASKED, i, :], -3e38))
            own.wait()
            tt(r_(SEL), r_(MASKED), r_(REPLACED), ALU.not_equal)
            own.wait()
            tt(r_(GATE), r_(SC), r_(SEL), ALU.mult)
            own.add(v.memset(rt[:, BEFORE, 0, :], 0.0))
            own.wait()
            for i in range(1, NT):
                tt(rt[:, BEFORE, i, :], rt[:, BEFORE, i - 1, :], rt[:, SEL, i - 1, :], ALU.add)
                own.wait()
            tt(cnt[:, 0, :], rt[:, BEFORE, NT - 1, :], rt[:, SEL, NT - 1, :], ALU.add)
            own.wait()
            v.engine_nop().then_inc(S("sel_ready"), 1)
            own.add(v.tensor_reduce(top[:, 1, :, 0], r_(GATE), AX_X, ALU.add))
            own.wait()
            own.add(v.reciprocal(top[:, 1, :, 1], top[:, 1, :, 0]))
            own.wait()
            tsc(top[:, 1, :, 1], top[:, 1, :, 1], SCALE_ROUTED, ALU.mult)
            own.wait()
            tt(r_(GATE), r_(GATE), bcast(top[:, 1, :, 1], 2, E), ALU.mult)
            flat_ = [rt[:, k].rearrange("p i e -> p (i e)") for k in (CUM, SEL)]
            own.add(v.tensor_tensor_scan(flat_[0], const[:, C_ONE:C_ONE + 1].to_broadcast([P, NT * E]), flat_[1],
                                         0.0, ALU.mult, ALU.add))
            own.wait()
            for i in range(NT):
                own.add(v.scalar_tensor_tensor(out=rt[:, RANK, i, :], in0=rt[:, CUM, i, :], scalar=float(-TOPK * i),
                                               in1=rt[:, SEL, i, :], op0=ALU.add, op1=ALU.mult))
            dve.wait_ge(S("pos_ready"), 1)
            off = (SLOTS - 1) / (2 * SLOTS)
            tsc(cnt[:, 2, :], psum[:, 0, 0:E], 1.0 / SLOTS, ALU.mult, (SLOTS - 1) / SLOTS - off, ALU.add)
            pos = psum[:, 3, :].rearrange("p (i e) -> p i e", i=NT)
            tsc(r_(DIV), pos, 1.0 / SLOTS, ALU.mult, -off, ALU.add)
            own.wait()
            for o in (cnt[:, 2, :], r_(DIV)):
                tsc(o, o, ROUND, ALU.add)
            own.wait()
            for o in (cnt[:, 2, :], r_(DIV)):
                tsc(o, o, ROUND, ALU.subtract)
            own.wait()
            own.add(v.tensor_tensor_scan(cnt[:, 3, :], const[:, C_ONE:C_ONE + 1].to_broadcast([P, E]), cnt[:, 2, :],
                                         0.0, ALU.mult, ALU.add))
            own.wait()
            tt(cnt[:, 4, :], cnt[:, 3, :], cnt[:, 2, :], ALU.subtract)
            own.wait()
            own.add(v.scalar_tensor_tensor(out=r_(DEST), in0=pos, scalar=float(MAXB), in1=bcast(cnt[:, 4, :], 1, NT),
                                           op0=ALU.mult, op1=ALU.add))
            own.wait()
            own.add(v.scalar_tensor_tensor(out=r_(DEST), in0=r_(DIV), scalar=float(1 - SLOTS * MAXB), in1=r_(DEST),
                                           op0=ALU.mult, op1=ALU.add))
            own.wait()
            v.engine_nop().then_inc(S("pos_taken"), 1)
            ranks = bcast(const[:, C_RANK:C_RANK + TOPK], 2, E)
            for i in range(NT):
                own.add(v.tensor_tensor(oh[:, 0], bcast(rt[:, RANK, i, :], 1, TOPK), ranks, ALU.is_equal))
                own.wait()
                for o, k in ((0, DEST), (1, GATE)):
                    tt(oh[:, 1], oh[:, 0], bcast(rt[:, k, i, :], 1, TOPK), ALU.mult)
                    own.wait()
                    own.add(v.tensor_reduce(dst[:, o, i, :], oh[:, 1], AX_X, ALU.add))
                    own.wait()
            own.add(v.tensor_copy(dsti[:], dst[:, 0]))
            own.add(v.tensor_copy(pay[:, :, :, 0], bcast(const[:, C_TOK:C_TOK + NT], 2, TOPK)))
            own.add(v.tensor_copy(pay[:, :, :, 1], dst[:, 1]))
            own.wait()
            v.engine_nop().then_inc(S("pay_ready"), 1)
            tsc(cnt[:, 5, :], cnt[:, 3, :], const[:, C_COL:C_COL + 1], ALU.is_le)
            own.wait()
            own.add(v.tensor_reduce(blk[:, 0:1], cnt[:, 5, :], AX_X, ALU.add))
            own.wait()
            tsc(blk[:, 0:1], blk[:, 0:1], float(E - 1), ALU.min)
            own.wait()
            tsc(blk[:, 1:2], blk[:, 0:1], 1.0 / RING, ALU.mult, -(RING - 1) / (2 * RING), ALU.add)
            own.wait()
            tsc(blk[:, 1:2], blk[:, 1:2], ROUND, ALU.add)
            own.wait()
            tsc(blk[:, 1:2], blk[:, 1:2], ROUND, ALU.subtract)
            own.wait()
            own.add(v.scalar_tensor_tensor(out=blk[:, 1:2], in0=blk[:, 1:2], scalar=float(-RING), in1=blk[:, 0:1],
                                           op0=ALU.mult, op1=ALU.add))
            tsc(cnt[:, 1, 0:1], cnt[:, 3, E - 1:E], 0.5, ALU.mult, 0.25, ALU.add)
            own.wait()
            v.engine_nop().then_inc(S("blk_ready"), 1)
            tsc(cnt[:, 1, 0:1], cnt[:, 1, 0:1], ROUND, ALU.add)
            own.wait()
            tsc(cnt[:, 1, 0:1], cnt[:, 1, 0:1], ROUND, ALU.subtract)
            own.wait()
            tsc(cnt[:, 1, 1:2], cnt[:, 1, 0:1], 2.0, ALU.subtract)
            own.wait()
            own.add(v.tensor_copy(ends[:, 0:E], cnt[:, 3, :]))
            own.add(v.tensor_copy(ends[:, E:E + 2], cnt[:, 1, 0:2]))

            for n in range(4):
                fc, th = n // 2, n % 2
                dve.wait_ge(S("shs_done"), n + 1)
                v.tensor_tensor(shT[:, fc, HALF * th:HALF * th + HALF], shs[:, n % 2, :],
                                psum[:, 5 + 2 * (n % 2), :], ALU.mult).then_inc(S("sh_taken"), 1)
            dve.wait_ge(S("rows_ready"), 1)
            own.add(v.tensor_copy(rows[0:2, 0:MAXB], psum[0:2, 3, 0:MAXB]))
            own.wait()
            v.engine_nop().then_inc(S("ends_ready"), 1)
            for i in range(NT):
                b = 2 * (i % 2)
                dve.wait_ge(S(f"ld_g{i % 2}"), 16 * (i // 2 + 1))
                dve.wait_ge(S("shd_ready"), i + 1)
                v.tensor_tensor(h1t[:, i % 2, :], h1t[:, i % 2, :],
                                psum[:, b:b + 2, :].rearrange("p k n -> p (k n)"), ALU.add)\
                    .then_inc(S("acc_done"), 1)

            dve.wait_ge(S("h2_stored"), 1)
            rounds = dve.value_load(ends[0:1, E + 1:E + 2], min_val=0, max_val=MAXB // 2 - 2)

            def take_x(t, b, early=False):
                dve.wait_ge(S("xt_ready"), t + 1)
                if not early:
                    dve.wait_ge(S("gu_ready"), t - 1)
                v.tensor_copy(xgT[:, b, 4:8, :].rearrange("p c s -> p (c s)"), psum[:, 1, :]).then_inc(S("xd"), 1)

            def hidden(t, b, early=False):
                dve.wait_ge(S("sgm_ready"), t + 1)
                if not early:
                    dve.wait_ge(S("hT_ready"), t - 1)
                v.tensor_tensor(hid[:, b, :], sgm[:, b, :], psum[:, 2 + b, F:2 * F], ALU.mult)\
                    .then_inc(S("hid_ready"), 1)

            def take_h(t, b, early=False):
                dve.wait_ge(S("hT_ready"), t + 1)
                if not early:
                    dve.wait_ge(S("y_made"), t)
                v.tensor_copy(hidT[:, b, :], psum[:, 4, 0:SLOTS]).then_inc(S("hT_taken"), 1)

            def take_y(t, b, early=False):
                dve.wait_ge(S("y_made"), t + 2)
                if not early:
                    dve.wait_ge(S("scattered"), 16 * t - 16)
                v.tensor_scalar(yb[:, b, HALF:D], psum[:, 6, :], tab[:, bass.ds(t, 1), 1:2].rearrange(
                    "p a b -> p (a b)"), None, ALU.mult).then_inc(S("yd"), 1)

            dve.wait_ge(S("table_read"), 16)
            take_x(0, 0, True)
            take_x(1, 1, True)
            hidden(0, 0, True)
            for k in range(2):
                t = 1 + k
                take_x(t + 1, k % 2)
                take_h(t - 1, k, True)
                hidden(t, (1 + k) % 2, t < 2)
                take_y(t - 1, k, True)
            with dve.Fori(1, dve.snap(rounds + 1)) as m:
                for k in range(2):
                    t = 2 * m + (1 + k)
                    take_x(t + 1, k)
                    take_h(t - 1, k)
                    hidden(t, (1 + k) % 2)
                    take_y(t - 1, k)
            last = dve.snap(2 * rounds + 3)
            take_h(last - 1, 0)
            hidden(last, 1)
            take_y(last - 1, 0)
            take_h(last, 1)
            take_y(last, 1)

            dve.wait_ge(S("moe_done"), 1)
            dve.wait_ge(S("ld_last"), 32)

            def evac_h(i):
                for j in range(2):
                    n = 2 * i + j
                    dve.wait_ge(S("ht_ready"), n + 1)
                    v.tensor_tensor(hpT[:, 4 * j:4 * j + 4, P * i:P * i + P],
                                    psum[:, n % 4, :].rearrange("p (c t) -> p c t", c=4),
                                    bcast(gcols[:, 2, 4 * j:4 * j + 4], 2, P), ALU.mult)\
                        .then_inc(S("hp_taken"), 1)

            def finish(i):
                dve.wait_ge(S("pg_done"), i + 1)
                dve.wait_ge(S(f"ld_j{i % 2}"), 16 * (i // 2 + 1))
                g = pg[:, i % 2, :]
                tt(g, g, prjt[:, i % 2, :], ALU.mult)
                own.wait()
                v.tensor_tensor(g, g, h2t[:, i % 3, :], ALU.add).then_inc(S("h3_done"), 1)
                dve.wait_ge(S("root4"), i + 1)
                own.add(v.reciprocal(stat[:, 5, i:i + 1], stat[:, 4, i:i + 1]))
                own.wait()
                v.scalar_tensor_tensor(out=ot[:, i % 2, :], in0=g, scalar=stat[:, 5, i:i + 1], in1=gfin[:],
                                       op0=ALU.mult, op1=ALU.mult).then_inc(S("out_done"), 1)

            for i in range(NT + 2):
                if i < NT:
                    dve.wait_ge(S("root3"), i + 1)
                    own.add(v.reciprocal(stat[:, 2, i:i + 1], stat[:, 1, i:i + 1]))
                    own.wait()
                    v.tensor_scalar(ht[:, i % 2, :], h2t[:, i % 3, :], stat[:, 2, i:i + 1], None, ALU.mult)\
                        .then_inc(S("hs_ready"), 1)
                    evac_h(i)
                if i >= 2:
                    finish(i - 2)

        @block.tensor
        def _(pe):
            mm = nc.tensor.matmul
            tr = nc.tensor.transpose

            pe.wait_ge(S("ld_const"), 32)
            for i in range(NT):
                pe.wait_ge(S("xs_ready"), i + 1)
                for j in range(2):
                    if i >= 1:
                        pe.wait_ge(S("xT_taken"), 2 * (i - 1) + j + 1)
                    for c in range(4):
                        ins = tr(psum[:, j, P * c:P * c + P], xin[i // 2][:, i % 2, P * (4 * j + c):P * (4 * j + c) + P], ident)
                    ins.then_inc(S("xT_ready"), 1)
            pe.wait_ge(S("xT_taken"), 2 * NT)
            pe.wait_ge(S("ld_wu"), 16)
            for k in range(STEP):
                if k >= 2:
                    pe.wait_ge(S("u_taken"), k - 1)
                for c in range(NC):
                    ins = mm(psum[:, 2 + k % 2, 0:SSM], xnT[:, c, k::STEP], wu[:, c, :],
                             start=(c == 0), stop=(c == NC - 1))
                ins.then_inc(S("u_ready"), 1)
            pe.wait_ge(S("u_taken"), STEP)
            for q in range(4):
                if q >= 2:
                    pe.wait_ge(S("Ug_taken"), q - 1)
                for g in range(4):
                    ins = tr(psum[:, 4 + q % 2, P * g:P * g + P],
                             ublk[:, 4 * q + g].rearrange("p s c -> p (s c)"), ident)
                ins.then_inc(S("Ut_ready"), 1)
            def project(i):
                b = 2 * (i % 2)
                if i >= 2:
                    pe.wait_ge(S("qkv_taken"), i - 1)
                for at, n, bank in ((0, QW, b), (QW, 2 * KVW, b + 1)):
                    for c in range(NC):
                        ins = mm(psum[:, bank, 0:n], xnT[:, c, P * i:P * i + P], wqkv[:, c, at:at + n],
                                 start=(c == 0), stop=(c == NC - 1))
                ins.then_inc(S("qkv_ready"), 1)
            pe.wait_ge(S("ld_wqkv"), 16)
            project(0)
            project(1)
            pe.wait_ge(S("vp_ready"), 1)
            pe.wait_ge(S("Ug_taken"), 4)
            for j in range(PAIRS):
                cols = slice(2 * CH * j, 2 * CH * j + 2 * CH)
                mm(psum[:, 4, cols], vp[:, 0, j], cblk[:, 0, j], start=True, stop=False)
                for r in range(2):
                    mm(psum[P - 2 * CH:P, 4, cols], bbz[:, r, j], cblk[:, r, PAIRS + j], start=False, stop=False)
                mm(psum[:, 4, cols], vp[:, 1, j], cblk[:, 1, j], start=False, stop=True)
                for r in range(2):
                    ins = mm(psum[:, 5, cols], vp[:, r, PAIRS + j], cblk[:, r, PAIRS + j], start=(r == 0),
                             stop=(r == 1))
            ins.then_inc(S("resp_ready"), 1)
            for k in range(8):
                d, r, q = k // 4, k // 2 % 2, k % 2
                if k >= 2:
                    pe.wait_ge(S("ws_taken"), k - 1)
                for j in range(4):
                    ins = tr(psum[:, 6 + k % 2, P * j:P * j + P],
                             vp[:, r, PAIRS * d + 4 * q + j], ident)
                ins.then_inc(S("ws_ready"), 1)
            pe.wait_ge(S("resp_taken"), 1)
            pe.wait_ge(S("ws_taken"), 8)
            for d in range(DIRS):
                if d:
                    pe.wait_ge(S("S_taken"), d)
                for r in range(2):
                    for j in range(PAIRS):
                        for gg in range(2):
                            u_ = Ug[:, 2 * j + gg, :] if d == 0 else Ug[:, 2 * j + gg, ::-1]
                            ins = mm(psum[ST * gg:ST * gg + ST, 4 + 2 * r + j // 4, P * (j % 4):P * (j % 4) + P],
                                     ws[:, d, r, j, ST * gg:ST * gg + ST], u_, start=True, stop=True)
                ins.then_inc(S("S_ready"), 1)
                for i in range(2 + 3 * d, 5 + 3 * d):
                    project(i)
            pe.wait_ge(S("qkv_taken"), NT)
            pe.wait_ge(S("X_ready"), DIRS)
            pe.wait_ge(S("T0_taken"), 1)
            for q in range(4):
                if q >= 2:
                    pe.wait_ge(S("y_taken"), q - 1)
                for gi in range(4):
                    g = 4 * q + gi
                    j, gg = g // 2, g % 2
                    rows_ = slice(ST * gg, ST * gg + ST)
                    o = psum[:, 2 * (q % 2) + gg, P * (gi // 2):P * (gi // 2) + P]
                    mm(o, t0[:, g, :], Ug[:, g, :], start=True, stop=False)
                    for d in range(DIRS):
                        for r in range(2):
                            x_ = xs[rows_, d, r, j, :] if d == 0 else xs[rows_, d, r, j, ::-1]
                            ins = mm(o, wy[rows_, r, PAIRS * d + j], x_, start=False, stop=(d == 1 and r == 1))
                ins.then_inc(S("y_ready"), 1)
            for q in range(4):
                pe.wait_ge(S("y_taken"), 4)
                if q >= 2:
                    pe.wait_ge(S("yk_taken"), q - 1)
                for gi in range(4):
                    ins = tr(psum[:, 2 + q % 2, P * gi:P * gi + P], yg[:, 4 * q + gi, :], ident)
                ins.then_inc(S("yk_ready"), 1)
            pe.wait_ge(S("yk_taken"), 4)
            for k in range(4):
                hh, q = k // 2, k % 2
                for t in range(4):
                    ins = tr(psum[:, 4 + k, P * t:P * t + P], ytok[:, 4 * q + t, P * hh:P * hh + P], ident)
                ins.then_inc(S("yT_ready"), 1)
            pe.wait_ge(S("ld_glu"), 32)
            pe.wait_ge(S("yT_taken"), 4)
            for k in range(4):
                co, th = k // 2, k % 2
                for c in range(2):
                    ins = mm(psum[:, k, :], wglu[:, c, P * co:P * co + P], yT[:, c, HALF * th:HALF * th + HALF],
                             start=(c == 0), stop=(c == 1))
                ins.then_inc(S("glu_ready"), 1)
            pe.wait_ge(S("glu_sig"), 4)
            for n in range(3 * NT):
                i, part = n // 3, n % 3
                pe.wait_ge(S("q_doubled") if part < 2 else S("k_doubled"), i + 1)
                if n >= 4:
                    pe.wait_ge(S("prep_taken"), n - 3)
                at, count = (4 * part, 4) if part < 2 else (HEADS, KV)
                for h in range(count):
                    ins = tr(psum[:, n % 4, P * h:P * h + P],
                             qkd[:, i % 2, at + h].rearrange("p a d -> p (a d)"), ident)
                ins.then_inc(S("prep_ready"), 1)
            pe.wait_ge(S("prep_taken"), 3 * NT)
            pe.wait_ge(S("KB_ones"), 1)

            def max_scores(h, i):
                m = 9 * h + i
                b = 2 * (m % 2)
                if m >= 2:
                    pe.wait_ge(S("max_taken"), m - 1)
                if i < NT:
                    for kh in range(2):
                        ins = mm(psum[:, b + kh, :], QA[0:HD, h, P * i:P * i + P],
                                 KB[0:HD, h // REP, HALF * kh:HALF * kh + HALF], start=True, stop=True)
                else:
                    pe.wait_ge(S("max_taken"), m)
                    ins = tr(psum[0:NT, b, 0:P], smax[:, h, :], ident)
                ins.then_inc(S("max_ready"), 1)

            def attend(n):
                h, qh, j = n // (2 * NT), n // NT % 2, n % NT
                pe.wait_ge(S("exp_done"), n + 1)
                if j == 0 and 2 * h + qh >= 2:
                    pe.wait_ge(S("O_taken"), 2 * h + qh - 1)
                at = HD * (h % 2)
                ins = mm(psum[:, 6 + (2 * h + qh) % 2, :], vaug[:, j, h // REP, at:at + 2 * HD],
                         pexp[:, n % 3, :], start=(j == 0), stop=(j == NT - 1))
                ins.then_inc(S("pv_done"), 1)

            for h in range(2):
                for i in range(NT + 1):
                    max_scores(h, i)
            steps = HEADS * 2 * NT
            for n in range(steps):
                h, qh, j = n // (2 * NT), n // NT % 2, n % NT
                if n % (2 * NT) == 0:
                    pe.wait_ge(S(f"mrow{h % 2}"), 16 * (h // 2 + 1))
                if n >= 2:
                    pe.wait_ge(S("exp_done"), n - 1)
                o = psum[:, 4 + n % 2, :]
                cols = slice(HALF * qh, HALF * qh + HALF)
                keys = slice(P * j, P * j + P)
                mm(o, KA[:, h // REP, keys], QA[:, h, cols], start=True, stop=False)
                mm(o, KB[0:HD + 1, h // REP, keys], QB[0:HD + 1, h, cols], start=False, stop=True)\
                    .then_inc(S("sT_ready"), 1)
                if n >= 1:
                    attend(n - 1)
                k = n % (2 * NT)
                if k % 2 == 1 and h + 2 < HEADS:
                    max_scores(h + 2, k // 2)
                if k == 2 * NT - 1 and h + 2 < HEADS:
                    max_scores(h + 2, NT)
            attend(steps - 1)

            pe.wait_ge(S("max_taken"), 9 * HEADS)
            pe.wait_ge(S("O_taken"), 2 * HEADS)
            for n in range(2 * NC):
                f_, th = n // 2, n % 2
                cols = slice(HALF * th, HALF * th + HALF)
                if th == 0:
                    pe.wait_ge(S(f"ld_m{f_ % 2}"), 64 * (f_ // 2 + 1))
                if n >= 2:
                    pe.wait_ge(S("mrg_taken"), n - 1)
                for k, (at, count, src) in enumerate(((0, 8, xnT), (16, 4, attnT), (8, 8, xnT), (20, 2, ssmT))):
                    for c in range(count):
                        ins = mm(psum[:, 4 * (n % 2) + k, :], wmrg[:, f_ % 2, at + c, :], src[:, c, cols],
                                 start=(c == 0), stop=(c == count - 1))
                ins.then_inc(S("mrg_ready"), 1)
            pe.wait_ge(S("mrg_taken"), 2 * NC)
            pe.wait_ge(S("ld_out"), 32)
            for i in range(NT + 1):
                if i < NT:
                    if i >= 2:
                        pe.wait_ge(S("h1_done"), i - 1)
                    for nh in range(2):
                        for c in range(NC):
                            ins = mm(psum[:, 2 * (i % 2) + nh, :], mergedT[:, c, P * i:P * i + P],
                                     wout[:, c, HALF * nh:HALF * nh + HALF], start=(c == 0), stop=(c == NC - 1))
                    ins.then_inc(S("wo_ready"), 1)
                if i >= 1:
                    pe.wait_ge(S("hn_done"), i)
                    for j in range(2):
                        n = 2 * (i - 1) + j
                        if n >= 4:
                            pe.wait_ge(S("hnT_taken"), n - 3)
                        for c in range(4):
                            at = P * (4 * j + c)
                            ins = tr(psum[:, 4 + n % 4, P * c:P * c + P], hntile[:, (i - 1) % 2, at:at + P], ident)
                        ins.then_inc(S("hnT_ready"), 1)
            pe.wait_ge(S("h1_done"), NT)
            pe.wait_ge(S("hnT_taken"), 2 * NT)
            pe.wait_ge(S("ld_router"), 32)
            for i in range(NT):
                for c in range(NC):
                    ins = mm(psum[:, 0, E * i:E * i + E], xnT[:, c, P * i:P * i + P], wrt[:, c, :],
                             start=(c == 0), stop=(c == NC - 1))
            ins.then_inc(S("lg_ready"), 1)
            for i in range(NT):
                pe.wait_ge(S(f"ld_p{i % 2}"), 16 * (i // 2 + 1))
                if i >= 2:
                    pe.wait_ge(S("pT_taken"), i - 1)
                for c in range(2):
                    ins = tr(psum[:, 1 + i % 2, P * c:P * c + P], ptok[:, i % 2, P * c:P * c + P], ident)
                ins.then_inc(S("pT_ready"), 1)
            pe.wait_ge(S("ld_wpp"), 16)
            for i in range(NT):
                pe.wait_ge(S("pT_taken"), i + 1)
                if i >= 2:
                    pe.wait_ge(S("prj_done"), i - 1)
                for nh in range(2):
                    for c in range(2):
                        ins = mm(psum[:, 4 + 2 * (i % 2) + nh, :], pT[:, c, P * i:P * i + P],
                                 wpp[:, c, HALF * nh:HALF * nh + HALF], start=(c == 0), stop=(c == 1))
                ins.then_inc(S("prj_ready"), 1)
            pe.wait_ge(S("sel_ready"), 1)
            pe.wait_ge(S("pT_taken"), NT)
            mm(psum[:, 3, :], const[:, C_TRI:C_TRI + P], rt[:, 4].rearrange("p i e -> p (i e)"),
               start=True, stop=False)
            mm(psum[:, 3, :], ones, rt[:, 6].rearrange("p i e -> p (i e)"), start=False, stop=True)
            mm(psum[:, 0, 0:E], ones, cnt[:, 0, :], start=True, stop=True).then_inc(S("pos_ready"), 1)
            pe.wait_ge(S("ld_wsh"), 48)
            pe.wait_ge(S("prj_done"), NT)
            for n in range(4):
                fc, th = n // 2, n % 2
                if n >= 2:
                    pe.wait_ge(S("sh_taken"), n - 1)
                for k in range(2):
                    for c in range(NC):
                        ins = mm(psum[:, 4 + 2 * (n % 2) + k, :], wsg[:, c, k, P * fc:P * fc + P],
                                 xnT[:, c, HALF * th:HALF * th + HALF], start=(c == 0), stop=(c == NC - 1))
                ins.then_inc(S("shgu_ready"), 1)
            pe.wait_ge(S("blk_ready"), 1)
            pe.wait_ge(S("pos_taken"), 1)
            tr(psum[0:2, 3, 0:P], blk[:, 0:2], ident).then_inc(S("rows_ready"), 1)
            pe.wait_ge(S("ends_ready"), 1)
            pe.wait_ge(S("sh_taken"), 4)
            for i in range(NT):
                if i >= 2:
                    pe.wait_ge(S("acc_done"), i - 1)
                for nh in range(2):
                    for c in range(2):
                        ins = mm(psum[:, 2 * (i % 2) + nh, :], shT[:, c, P * i:P * i + P],
                                 wsd[:, c, HALF * nh:HALF * nh + HALF], start=(c == 0), stop=(c == 1))
                ins.then_inc(S("shd_ready"), 1)

            pe.wait_ge(S("acc_done"), NT)
            rounds = pe.value_load(ends[0:1, E + 1:E + 2], min_val=0, max_val=MAXB // 2 - 2)

            def turn_x(t, b, count, early=False):
                pe.wait_ge(S(f"gathered{b}"), 16 * count + 16)
                if not early:
                    pe.wait_ge(S("xa"), t)
                    pe.wait_ge(S("xd"), t)
                for c in range(NC):
                    ins = tr(psum[:, c // 4, P * (c % 4):P * (c % 4) + P], xg[:, b, P * c:P * c + P], ident)
                ins.then_inc(S("xt_ready"), 1)

            def gate_up(t, b, early=False):
                expert = pe.value_load(rows[0:1, bass.ds(t, 1)], min_val=0, max_val=E - 1)
                slot = pe.value_load(rows[1:2, bass.ds(t, 1)], min_val=0, max_val=RING - 1)
                pe.wait_ge(S("w_ready"), expert + 1)
                pe.wait_ge(S("xa"), t + 1)
                pe.wait_ge(S("xd"), t + 1)
                if not early:
                    pe.wait_ge(S("hid_ready"), t - 1)
                for c in range(NC):
                    ins = mm(psum[:, 2 + b, 0:2 * F], xgT[:, b, c, :],
                             wexp[:, bass.ds(slot, 1), 2 * F * c:2 * F * c + 2 * F].rearrange("p a n -> p (a n)"),
                             start=(c == 0), stop=(c == NC - 1))
                ins.then_inc(S("gu_ready"), 1)

            def turn_h(t, b, early=False):
                pe.wait_ge(S("hid_ready"), t + 1)
                if not early:
                    pe.wait_ge(S("hT_taken"), t)
                tr(psum[:, 4, 0:SLOTS], hid[:, b, :], ident).then_inc(S("hT_ready"), 1)

            def down(t, b, early=False):
                slot = pe.value_load(rows[1:2, bass.ds(t, 1)], min_val=0, max_val=RING - 1)
                pe.wait_ge(S("hT_taken"), t + 1)
                if not early:
                    pe.wait_ge(S("ya"), t)
                    pe.wait_ge(S("yd"), t)
                for nh in range(2):
                    at = NC * 2 * F + HALF * nh
                    ins = mm(psum[:, 5 + nh, :], hidT[:, b, :],
                             wexp[:, bass.ds(slot, 1), at:at + HALF].rearrange("p a n -> p (a n)"),
                             start=True, stop=True)
                ins.then_inc(S("y_made"), 1)

            pe.nop().then_inc(S("y_made"), 1)
            turn_x(0, 0, 0, True)
            turn_x(1, 1, 0)
            gate_up(0, 0, True)
            for k in range(2):
                t = 1 + k
                turn_x(t + 1, k, 1)
                turn_h(t - 1, k, t == 1)
                gate_up(t, (1 + k) % 2, t < 2)
                down(t - 1, k, t == 1)
            with pe.Fori(1, pe.snap(rounds + 1)) as m:
                for k in range(2):
                    t = 2 * m + (1 + k)
                    turn_x(t + 1, k, m + 1)
                    turn_h(t - 1, k)
                    gate_up(t, (1 + k) % 2)
                    down(t - 1, k)
            last = pe.snap(2 * rounds + 3)
            turn_h(last - 1, 0)
            gate_up(last, 1)
            down(last - 1, 0)
            turn_h(last, 1)
            down(last, 1)

            pe.wait_ge(S("moe_done"), 1)
            pe.wait_ge(S("ld_last"), 32)
            for i in range(NT + 1):
                if i < NT:
                    pe.wait_ge(S("hs_ready"), i + 1)
                    for j in range(2):
                        n = 2 * i + j
                        if n >= 4:
                            pe.wait_ge(S("hp_taken"), n - 3)
                        for c in range(4):
                            at = P * (4 * j + c)
                            ins = tr(psum[:, n % 4, P * c:P * c + P], ht[:, i % 2, at:at + P], ident)
                        ins.then_inc(S("ht_ready"), 1)
                if i >= 1:
                    k = i - 1
                    pe.wait_ge(S("hp_taken"), 2 * k + 2)
                    if k >= 2:
                        pe.wait_ge(S("pg_done"), k - 1)
                    for nh in range(2):
                        for c in range(NC):
                            ins = mm(psum[:, 4 + 2 * (k % 2) + nh, :], hpT[:, c, P * k:P * k + P],
                                     wpg[:, c, HALF * nh:HALF * nh + HALF], start=(c == 0), stop=(c == NC - 1))
                    ins.then_inc(S("pg_ready"), 1)


def constants():
    c = np.zeros((P, C_END), np.float32)
    c[:, C_ID:C_ID + P] = np.eye(P)
    c[:, C_TRI:C_TRI + P] = np.triu(np.ones((P, P)), 1)
    t = np.arange(T)
    inv = (10000.0 ** (-np.arange(0, HD // 2, 2, dtype=np.float32) / (HD // 2))).astype(np.float32)
    ang = np.stack([(t // GRID_W)[:, None] * inv, (t % GRID_W)[:, None] * inv], 1).astype(np.float32)
    ang = ang.astype(np.float64)
    cos = np.stack([np.cos(ang), np.cos(ang)], 2).reshape(NT, P, HD)
    sin = np.stack([-np.sin(ang), np.sin(ang)], 2).reshape(NT, P, HD)
    c[:, C_COS:C_COS + NT * HD] = cos.transpose(1, 0, 2).reshape(P, -1)
    c[:, C_SIN:C_SIN + NT * HD] = sin.transpose(1, 0, 2).reshape(P, -1)
    c[:, C_TOK:C_TOK + NT] = t.reshape(NT, P).T
    c[:, C_COL] = np.arange(P)
    c[:, C_LOW:C_LOW + EG * EG] = np.tril(np.ones((EG, EG)), -1).reshape(-1)
    c[:, C_RANK:C_RANK + TOPK] = np.arange(1, TOPK + 1)
    c[:, C_ONE:C_ONE + P] = 1.0
    return c


def layout(a):
    a = {k: np.asarray(v) for k, v in a.items()}

    def cols(g):
        return g.reshape(-1, P).T

    def states(v):
        v = v.reshape(DIRS, PAIRS, 2, ST, *v.shape[3:])
        return np.moveaxis(v, (2, 3, 0, 1), (0, 1, 2, 3)).reshape(P, DP, *v.shape[4:])

    log_dt = np.broadcast_to(a["log_dt"][0][:, :, None], (DIRS, GROUPS, ST))
    gate = a["w_exp_gate"][0].reshape(E, NC, P, F)
    up = a["w_exp_up"][0].reshape(E, NC, P, F)
    gu = np.stack([gate, up], 3).transpose(0, 2, 1, 3, 4).reshape(E, P, NC * 2 * F)
    r = {
        "const": constants(),
        "gcols": np.stack([cols(a["g_mix"][0]), cols(a["g_ffn"][0]), cols(a["g_ple"][0])], 1),
        "ssm_par": np.stack([states(a["a_re"][0]), states(a["a_im"][0]), states(log_dt)], 1),
        "ssm_bc": np.stack([states(a["b_re"][0]), states(a["b_im"][0]),
                            states(a["c_re"][0].transpose(0, 1, 3, 2)),
                            states(a["c_im"][0].transpose(0, 1, 3, 2))], 1),
        "d_skip": np.broadcast_to(a["d_skip"][0].reshape(1, GROUPS, CH), (STEP, GROUPS, CH))
        .transpose(0, 2, 1).reshape(P, GROUPS),
        "b_glu": cols(a["b_glu"][0]),
        "w_exp": np.concatenate([gu, a["w_exp_down"][0]], 2),
        "x": a["x"][0], "p": a["p"][0, 0], "g_final": a["g_final"],
    }
    for k in ("w_in", "q_norm", "k_norm", "w_attn_up", "w_glu", "w_ssm_up", "w_out", "g_ffn", "w_router",
              "router_bias", "w_sh_gate", "w_sh_up", "w_sh_down", "w_ple_gate", "w_ple_proj"):
        r[k] = a[k][0]
    return {k: np.ascontiguousarray(v) for k, v in r.items()}


def kernel(**inputs):
    import concourse.bacc as bacc
    from concourse.bass_utils import run_bass_kernel_spmd

    nc = bacc.Bacc("TRN2", target_bir_lowering=False, num_devices=1)
    arrays = {f"in_{k}": v for k, v in layout(inputs).items()}
    A = {k[3:]: nc.dram_tensor(k, v.shape, mybir.dt.from_np(v.dtype), kind="ExternalInput").ap()
         for k, v in arrays.items()}
    out = nc.dram_tensor("out", (T, D), F32, kind="ExternalOutput").ap()
    build(nc, A, out)
    r = run_bass_kernel_spmd(nc, [arrays], core_ids=[0])
    return r.results[0]["out"].reshape(1, T, D)
```

```python
from contextlib import ExitStack

import numpy as np

import concourse.bass as bass
from concourse import mybir

F32 = mybir.dt.float32
F32R = mybir.dt.float32r
I32 = mybir.dt.int32
ALU = mybir.AluOpType
ACT = mybir.ActivationFunctionType
AX_X = mybir.AxisListType.X

P = 128
T = 1024
D = 1024
NT = T // P
NC = D // P
HALF = 512
EPS = 1e-6
GRID_W = 64

HEADS, KV, HD = 8, 2, 64
QW, KVW = HEADS * HD, KV * HD
REP = HEADS // KV
SSM = 256
GROUPS, CH, ST = 16, 16, 64
PAIRS = GROUPS // 2
DIRS = 2
DP = DIRS * PAIRS
STEP = 8
NBLK = T // STEP
GATE_A = QW + 2 * KVW + SSM
GATE_S = GATE_A + D

E, F = 64, 128
TOPK, EG, GE, TOPG = 8, 8, 8, 4
SLOTS = P
MAXB = P
AHEAD = 3
SKIP = 4096
RING = 4
SH = 256
PLE = 256
SCALE_ROUTED = 2.5
TWO_PI = 2.0 * np.pi
ROUND = float(3 << 22)

C_ID = 0
C_TRI = C_ID + P
C_COS = C_TRI + P
C_SIN = C_COS + NT * HD
C_TOK = C_SIN + NT * HD
C_COL = C_TOK + NT
C_LOW = C_COL + 1
C_RANK = C_LOW + EG * EG
C_ONE = C_RANK + TOPK
C_IOTA = C_ONE + P
C_END = C_IOTA + P


MAX_STEPS = tuple(range(3, 3 + NT)) + (NT + 3,)
WOUT_PARTS = ((0, 2), (2, 4), (4, NC))
GATE_SPLITS = 2 * NC


def split_no(f=None, c=None):
    if c is not None:
        return 2 + c
    return 1 if f == 0 else NC + 1 + f


class Order:

    def __init__(self, eng, sem):
        self.eng, self.sem, self.n = eng, sem, 0

    def add(self, ins):
        ins.then_inc(self.sem, 1)
        self.n += 1

    def wait(self):
        self.eng.wait_ge(self.sem, self.n)


def bcast(ap, axis, n):
    a = ap.unsqueeze(axis)
    shape = list(a.shape)
    shape[axis] = n
    return a.to_broadcast(shape)


def build(nc, A, out):
    ctx = ExitStack()
    pool, at = [], {}

    def sb(name, shape, dt=F32):
        cm = nc.sbuf_tensor(name, shape, dt)
        pool.append(cm)
        tile = cm.__enter__()
        at[name] = nc.sbuf_base - int(np.prod(shape[1:])) * mybir.dt.size(dt)
        return tile

    def split_over(name, tile, shape):
        return nc.alloc_sbuf_tensor_at(name, shape, F32R, offset=at[tile])

    def free_to(n):
        while len(pool) > n:
            pool.pop().__exit__(None, None, None)

    def dram(name, shape, dt=F32):
        return nc.dram_tensor(name, shape, dt, kind="Internal").ap()

    sems = {}

    def S(name):
        if name not in sems:
            sems[name] = ctx.enter_context(nc.semaphore(name))
        return sems[name]

    with ctx:
        psum = ctx.enter_context(nc.psum_tensor("psum", [P, 8, HALF], F32))
        hn_rows = dram("hn_rows", [T, D])
        h1_rows = dram("h1_rows", [T, D])
        h2_rows = dram("h2_rows", [T, D])
        prj_rows = dram("prj_rows", [T, D])

        const = sb("const", [P, C_END])
        ident = const[:, C_ID:C_ID + P]
        ones = const[:, C_ONE:C_ONE + P]
        gcols = sb("gcols", [P, NC])
        stat = sb("stat", [P, 6, NT])
        xnT = sb("xnT", [P, NC, T])
        wrt = sb("wrt", [P, NC, E])
        rbias = sb("rbias", [P, E])
        base = len(pool)

        ssmT = sb("ssmT", [P, 2, T])
        qk = sb("qk", [P, NT, QW + KVW])
        merge_from = len(pool)
        vaug = sb("vaug", [P, NT, KV, 3 * HD])
        rope = sb("rope", [P, 4, NT, HD])
        qkss = sb("qkss", [P, 3, NT, HEADS + KV])
        nrmw = sb("nrmw", [P, 2, HD])
        sb("pad", [P, 400])
        pool_from = len(pool)

        wqkv = sb("wqkv", [P, NC, QW + 2 * KVW])
        wsu = sb("wsu", [P, DIRS * 2 * PAIRS * P])
        xt = sb("xt", [P, 2, D])
        ublk = sb("ublk", [P, GROUPS, STEP, CH])
        Ug = sb("Ug", [P, GROUPS, NBLK])
        par = sb("par", [P, 3, DP])
        sp = sb("sp", [P, 16, DP])
        bc = sb("bc", [P, 4, DP, CH])
        bb = sb("bb", [P, 2, DP, CH])
        pw = sb("pw", [P, 2, DP, STEP + 1])
        vp = sb("vp", [P, 2, DP, STEP, CH])
        bbz = sb("bbz", [P, 2, PAIRS, 2, CH])
        wy = sb("wy", [P, 2, DP, STEP, CH])
        cblk = sb("cblk", [P, 2, DP, 2, CH])
        dskip = sb("dskip", [P, GROUPS])
        wglu = sb("wglu", [P, 2, SSM])
        bglu = sb("bglu", [P, 2])
        qflat, vflat = qk[:].rearrange("p i n -> p (i n)"), vaug[:].rearrange("p i g n -> p (i g n)")
        xin = [a.rearrange("p (i d) -> p i d", d=D) for a in
               (qflat[:, 0:2 * D], qflat[:, 2 * D:4 * D], xt[:].rearrange("p i d -> p (i d)"), vflat[:, 0:2 * D])]
        tmp = xt
        wu = wsu[:, 0:NC * SSM].rearrange("p (c n) -> p c n", c=NC)
        ws = wsu[:].rearrange("p (d r j m) -> p d r j m", d=DIRS, r=2, j=PAIRS)
        xs = ws
        t0 = ssmT[:].rearrange("p c t -> p (c t)").rearrange("p (g m) -> p g m", g=GROUPS)
        wrot = rope[:].rearrange("p a i d -> p (a i d)").rearrange("p (r j b) -> p r j b", r=2, j=PAIRS)
        resp = rope[:].rearrange("p a i d -> p (a i d)")[:, 0:2 * SSM].rearrange("p (d n) -> p d n", d=2)
        stage = ublk[:].rearrange("p g s c -> p (g s c)").rearrange("p (t n) -> p t n", t=STEP)
        flat = vp[:].rearrange("p r q e c -> p (r q e c)")
        rot = flat.rearrange("p (r q b) -> p r q b", r=2, q=DP)
        yg = ublk[:].rearrange("p g s c -> p g (s c)")
        ytok = Ug[:].rearrange("p g b -> p (g b)").rearrange("p (s c) -> p s c", s=STEP)
        yT = tmp[:]
        sglu = flat[:, 0:2 * T].rearrange("p (r n) -> p r n", r=2)
        qtmp = flat[:, 2 * T:4 * T].rearrange("p (k n) -> p k n", k=2)
        free_to(pool_from)

        qkd = sb("qkd", [P, 2, HEADS + KV, 2, HD])
        QA = sb("QA", [P, HEADS, T], F32R)
        QB = sb("QB", [P, HEADS, T], F32R)
        KA = sb("KA", [P, KV, T], F32R)
        KB = sb("KB", [P, KV, T], F32R)
        pexp = sb("pexp", [P, 3, HALF])
        smax = sb("smax", [P, HEADS, NT])
        smaxT = sb("smaxT", [NT, HEADS, P], F32R)
        rsum = sb("rsum", [P, 2, HALF])
        attnT = qk[:].rearrange("p i n -> p (i n)")[:, 0:4 * T].rearrange("p (c t) -> p c t", c=4)
        free_to(merge_from)

        sg = sb("sg", [P, 2, 2, HALF])
        gffn = sb("gffn", [P, D])
        wm = [sb("wm0", [P, 22, P]), sb("wm1", [P, 22, P])]
        mergedT = sb("mergedT", [P, NC, T])
        wout = sb("wout", [P, NC, D])
        xh, xl = split_over("xh", "wout", [P, NC, T]), split_over("xl", "xnT", [P, NC, T])
        htile = sb("htile", [P, 3, D])
        hntile = sb("hntile", [P, 2, D])
        ptok = sb("ptok", [P, NT, PLE])
        wpp = sb("wpp", [P, 2, D])
        wh = [split_over("wh0", "ptok", [P, 2 * NC, P]), split_over("wh1", "wpp", [P, 2 * NC, P])]
        wl = [split_over("wl0", "wm0", [P, 2 * NC, P]), split_over("wl1", "wm1", [P, 2 * NC, P])]
        free_to(base)

        wexp = sb("wexp", [P, RING, NC * 2 * F + D])
        tab = sb("tab", [P, 2, MAXB + AHEAD])
        rows = sb("rows", [P, 2 * P], I32)
        ends = sb("ends", [P, E + 2], I32)
        idx = sb("idx", [P, 4], I32)
        xg = sb("xg", [P, 2, D])
        xgT = sb("xgT", [P, 2, NC, P])
        moe_from = len(pool)
        wsg = sb("wsg", [P, NC, 2, SH])
        wsd = sb("wsd", [P, 2, D])
        pT = sb("pT", [P, 2, T])
        prj = sb("prj", [P, 2, D])
        rt = sb("rt", [P, 10, NT, E])
        oh = sb("oh", [P, 2, TOPK, E])
        grp = sb("grp", [P, 4, NT, EG])
        cmp = sb("cmp", [P, 3, NT, EG * EG])
        dst = sb("dst", [P, 4, NT, TOPK])
        blk_hot = sb("blk_hot", [P, 4, 2, MAXB])
        slot_hot = sb("slot_hot", [P, 4, SLOTS])
        top = sb("top", [P, 2, NT, TOPK])
        blk = sb("blk", [P, 4])
        cnt = sb("cnt", [P, 6, E])
        shT = sb("shT", [P, 2, T])
        shs = sb("shs", [P, 2, HALF])
        h1t = sb("h1t", [P, 2, D])
        h1p = [h1t, prj]
        free_to(moe_from)
        wpg = sb("wpg", [P, NC, D])
        gfin = sb("gfin", [P, D])
        gple = sb("gple", [P, D])
        loop_from = len(pool)
        sgm = sb("sgm", [P, 2, F])
        hid = sb("hid", [P, 2, F])
        hidT = sb("hidT", [P, 2, SLOTS])
        yb = sb("yb", [P, 2, D])
        free_to(loop_from)
        h2t = sb("h2t", [P, 5, D])
        ht = sb("ht", [P, 2, D])
        pg = sb("pg", [P, 2, D])
        prjt = sb("prjt", [P, 2, D])
        hp_hi, hp_lo = split_over("hp_hi", "xgT", [P, 2, NC, P]), split_over("hp_lo", "xg", [P, 2, NC, P])
        wpg_hi, wpg_lo = split_over("wpg_hi", "xnT", [P, NC, D]), split_over("wpg_lo", "wpg", [P, NC, D])
        free_to(base)
        free_to(0)

        block = ctx.enter_context(nc.Block())

        @block.sync
        def _(sp_):
            dma = sp_.dma_start
            dma(xin[0][:, 0, :], A["x"][0:P]).then_inc(S("ld_xfirst"), 16)
            dma(const[:], A["const"]).then_inc(S("ld_const"), 16)
            dma(gcols[:], A["gcols"]).then_inc(S("ld_const"), 16)
            dma(xin[0][:, 1, :], A["x"][P:2 * P]).then_inc(S("ld_x0"), 16)
            dma(par[:], A["ssm_par"]).then_inc(S("ld_ssm"), 16)
            dma(bc[:], A["ssm_bc"]).then_inc(S("ld_ssm"), 16)
            dma(dskip[:], A["d_skip"]).then_inc(S("ld_ssm"), 16)
            dma(nrmw[:, 0, :], A["q_norm"].partition_broadcast(P)).then_inc(S("ld_norms"), 16)
            dma(nrmw[:, 1, :], A["k_norm"].partition_broadcast(P)).then_inc(S("ld_norms"), 16)
            for k in range(1, NT // 2):
                dma(xin[k], A["x"][2 * P * k:2 * P * k + 2 * P].rearrange("(i p) d -> p i d", p=P))\
                    .then_inc(S(f"ld_x{k}"), 16)
                if k == 2:
                    dma(wu, A["w_u"]).then_inc(S("ld_wu"), 16)
            dma(wqkv[:], A["w_qkv"]).then_inc(S("ld_wqkv"), 16)
            dma(wglu[:], A["w_glu"].rearrange("(k p) n -> p k n", p=P)).then_inc(S("ld_glu"), 16)
            dma(bglu[:], A["b_glu"]).then_inc(S("ld_glu"), 16)
            dma(wrt[:], A["w_router"].rearrange("(c p) n -> p c n", p=P)).then_inc(S("ld_router"), 16)
            dma(rbias[:], A["router_bias"].partition_broadcast(P)).then_inc(S("ld_router"), 16)
            sp_.wait_ge(S("resp_taken"), 1)
            for t in range(STEP):
                n = CH * (t + 1)
                dma(stage[0:n, t, :], resp[P - n:P, 0, :]).then_inc(S("T0_ready"), 16)
                if n < P:
                    dma(stage[n:P, t, :], resp[CH:CH + P - n, 1, :]).then_inc(S("T0_ready"), 16)
            def load_chunk(f_):
                dma(wm[f_ % 2][:], A["w_merge"][f_]).then_inc(S(f"ld_m{f_ % 2}"), 16)

            for h in range(HEADS):
                if h == HEADS - 2:
                    load_chunk(0)
                sp_.wait_ge(S("max_taken"), 9 * h + 9)
                dma(QB[HD:HD + 1, h, :].bitcast(F32), smaxT[:, h, :].bitcast(F32)).then_inc(S(f"mrow{h % 2}"), 16)

            sp_.wait_ge(S("O_taken"), 2 * HEADS)
            x_tiles = A["x"].rearrange("(i p) d -> i p d", p=P)
            h1_tiles = h1_rows.rearrange("(i p) d -> i p d", p=P)
            hn_tiles = hn_rows.rearrange("(i p) d -> i p d", p=P)
            h2_tiles = h2_rows.rearrange("(i p) d -> i p d", p=P)
            for f_ in range(NC):
                if f_ >= 2:
                    sp_.wait_ge(S("mrg_ready"), 2 * (f_ - 1))
                if f_ >= 1:
                    load_chunk(f_)
                if f_ == 1:
                    dma(gffn[:], A["g_ffn"].partition_broadcast(P)).then_inc(S("ld_out0"), 16)
                    for i in range(3):
                        dma(htile[:, i, :], x_tiles[i]).then_inc(S(f"ld_h{i}"), 16)
            sp_.wait_ge(S("mrg_ready"), 2 * NC)
            w_ = A["w_out"].rearrange("(c p) n -> p c n", p=P)
            for k, (lo, hi) in enumerate(WOUT_PARTS):
                dma(wout[:, lo:hi], w_[:, lo:hi]).then_inc(S(f"ld_out{k}"), 16)
            dma(ptok[:], A["p"].rearrange("(i p) d -> p i d", p=P)).then_inc(S("ld_p"), 16)
            dma(wpp[:], A["w_ple_proj"].rearrange("(c p) n -> p c n", p=P)).then_inc(S("ld_p"), 16)
            for i in range(NT):
                sp_.wait_ge(S("h1_done"), i + 1)
                dma(h1_tiles[i], htile[:, i % 3, :]).then_inc(S("st_h1"), 16)
                sp_.wait_ge(S("hn_done"), i + 1)
                dma(hn_tiles[i], hntile[:, i % 2, :]).then_inc(S("st_hn"), 16)
                sp_.wait_ge(S("st_h1"), 16 * (i + 1))
                sp_.wait_ge(S("st_hn"), 16 * (i + 1))
                sp_.nop().then_inc(S("h_stored"), 1)
                if i + 3 < NT:
                    dma(htile[:, i % 3, :], x_tiles[i + 3]).then_inc(S(f"ld_h{i % 3}"), 16)

            sp_.wait_ge(S("hnT_taken"), 2 * NT)
            prj_tiles = prj_rows.rearrange("(i p) d -> i p d", p=P)
            dma(wsg[:], A["w_sh_gate_up"]).then_inc(S("ld_wsh"), 16)
            dma(wsd[:], A["w_sh_down"].rearrange("(c p) n -> p c n", p=P)).then_inc(S("ld_wsh"), 16)
            for i in range(NT):
                sp_.wait_ge(S("prj_done"), i + 1)
                dma(prj_tiles[i], prj[:, i % 2, :]).then_inc(S(f"st_prj{i % 2}"), 16)
            h1_pairs = h1_rows.rearrange("(k i p) d -> k p i d", p=P, i=2)
            for k in range(2):
                sp_.wait_ge(S(f"st_prj{k}"), 16 * (NT // 2))
            for k in range(2):
                dma(h1p[k][:], h1_pairs[k]).then_inc(S(f"ld_g{k}"), 16)
            for e in range(RING):
                dma(wexp[:, e, :], A["w_exp"][e]).then_inc(S(f"ld_w{e}"), 16)
            for i in range(NT):
                k = i // 2
                sp_.wait_ge(S("acc_done"), i + 1)
                dma(h2_tiles[i], h1p[k % 2][:, i % 2, :]).then_inc(S(f"st_h2{i % 2}"), 16)
                if i % 2 == 1 and k + 2 < NT // 2:
                    for n in range(2):
                        sp_.wait_ge(S(f"st_h2{n}"), 16 * (k + 1))
                    dma(h1p[k % 2][:], h1_pairs[k + 2]).then_inc(S(f"ld_g{k % 2}"), 16)
            for k in range(2):
                sp_.wait_ge(S(f"st_h2{k}"), 16 * (NT // 2))
            sp_.nop().then_inc(S("h2_stored"), 1)

            sp_.wait_ge(S("ends_ready"), 1)
            for e in range(RING - 1):
                sp_.wait_ge(S(f"ld_w{e}"), 16)
                sp_.nop().then_inc(S("w_ready"), 1)
            dma(gfin[:], A["g_final"].partition_broadcast(P)).then_inc(S("ld_last"), 16)
            dma(gple[:], A["g_ple"].partition_broadcast(P)).then_inc(S("ld_last"), 16)
            wpg_parts = wpg[:].rearrange("p c n -> p (c n)").rearrange("p (q n) -> p q n", q=E // RING)
            dma(wpg_parts[:, 0, :], A["w_ple_gate"][0]).then_inc(S("ld_last"), 16)
            with sp_.Fori(1, E // RING) as q:
                dma(wpg_parts[:, bass.ds(q, 1), :].rearrange("p a n -> p (a n)"),
                    A["w_ple_gate"][bass.ds(q, 1)].rearrange("q p n -> p (q n)")).then_inc(S("ld_last"), 16)
                for r in range(RING):
                    last = sp_.value_load(ends[0:1, bass.ds(RING * q + (r - RING), 1)], min_val=0, max_val=MAXB)
                    sp_.wait_ge(S("y_made"), last + 1)
                    dma(wexp[:, r, :], A["w_exp"][bass.ds(RING * q + r, 1)].rearrange("e p n -> p (e n)"))\
                        .then_inc(S(f"ld_w{r}"), 16)
                    k = (r - 1) % RING
                    sp_.wait_ge(S(f"ld_w{k}"), 16 * q + (16 if r >= 1 else 0))
                    sp_.nop().then_inc(S("w_ready"), 1)
            for e in range(E - 1, E):
                sp_.wait_ge(S(f"ld_w{e % RING}"), 16 * (E // RING))
                sp_.nop().then_inc(S("w_ready"), 1)

            sp_.wait_ge(S("moe_done"), 1)
            for i in range(5):
                dma(h2t[:, i, :], h2_tiles[i]).then_inc(S(f"ld_e{i}"), 16)
                if 1 <= i < 3:
                    dma(prjt[:, i - 1, :], prj_tiles[i - 1]).then_inc(S(f"ld_j{i - 1}"), 16)
            out_tiles = out.rearrange("(i p) d -> i p d", p=P)
            for i in range(NT):
                sp_.wait_ge(S("out_done"), i + 1)
                dma(out_tiles[i], pg[:, i % 2, :]).then_inc(S(f"st_out{i % 2}"), 16)
                if i + 5 < NT:
                    dma(h2t[:, i % 5, :], h2_tiles[i + 5]).then_inc(S(f"ld_e{i % 5}"), 16)
                if i + 2 < NT:
                    dma(prjt[:, i % 2, :], prj_tiles[i + 2]).then_inc(S(f"ld_j{i % 2}"), 16)
            for k in range(2):
                sp_.wait_ge(S(f"st_out{k}"), 16 * (NT // 2))

        @block.gpsimd
        def _(pool_):
            nc.gpsimd.memset(bbz[:], 0.0).then_inc(S("tile_set"), 1)
            nc.gpsimd.memset(cblk[:], 0.0).then_inc(S("tile_set"), 1)
            pool_.wait_ge(S("xT_ready"), 2 * NT)
            nc.gpsimd.memset(vaug[:], 1.0).then_inc(S("tile_set"), 1)
            pool_.wait_ge(S("ssm_done"), 1)
            nc.gpsimd.memset(KB[HD:HD + 1].bitcast(F32), 1.0).then_inc(S("KB_ones"), 1)
            pool_.wait_ge(S("KB_ones"), 1)
            for i in range(NT):
                pool_.wait_ge(S("qk_ready"), i + 1)
                if i >= 2:
                    pool_.wait_ge(S("prep_ready"), 3 * (i - 1))
                nc.gpsimd.tensor_copy(qkd[:, i % 2, HEADS:],
                                      bcast(qk[:, i, QW:].rearrange("p (h d) -> p h d", d=HD), 2, 2))\
                    .then_inc(S("k_doubled"), 1)

            pool_.wait_ge(S("hnT_taken"), 2 * NT)
            nc.gpsimd.memset(tab[:, 0, MAXB:], float(SKIP)).then_inc(S("tile_set"), 1)
            nc.gpsimd.memset(tab[:, 1, MAXB:], 0.0).then_inc(S("tile_set"), 1)
            nc.gpsimd.memset(xg[:], 0.0).then_inc(S("tile_set"), 1)
            pool_.wait_ge(S("dest_ready"), 1)
            for n in range(NT * TOPK):
                if n >= 4:
                    pool_.wait_ge(S("hot_used"), n - 3)
                nc.gpsimd.tensor_scalar(slot_hot[:, n % 4, :], const[:, C_IOTA:C_IOTA + P],
                                        dst[:, 3, n // TOPK, n % TOPK:n % TOPK + 1], None, ALU.is_equal)\
                    .then_inc(S("slot_hot"), 1)
            pool_.wait_ge(S("tab_ready"), 1)
            pool_.wait_ge(S("tile_set"), 6)


            def gather(t, b):
                nc.gpsimd.tensor_copy(idx[:, b:b + 1], tab[:, 0, bass.ds(t, 1)])\
                    .then_inc(S("gidx"), 1)
                pool_.wait_ge(S("gidx"), t + 1)
                pool_.nop().then_inc(S("pool_turn"), 1)
                pool_.indirect_dma_start(xg[:, b, :], None, hn_rows, bass.IndirectOffsetOnAxis(idx[:, b:b + 1], 0),
                                         bounds_check=T - 1, oob_is_err=False).then_inc(S(f"gathered{b}"), 16)

            def scatter(t, b, early=False):
                nc.gpsimd.tensor_copy(idx[:, 2 + b:3 + b],
                                      tab[:, 0, bass.ds(t, 1)])\
                    .then_inc(S("sidx"), 1)
                pool_.wait_ge(S("sidx"), t + 1)
                pool_.wait_ge(S("ya"), t + 1)
                pool_.wait_ge(S("yd"), t + 1)
                if not early:
                    pool_.wait_ge(S("scattered"), 16 * t)
                pool_.nop().then_inc(S("pool_turn"), 1)
                pool_.indirect_dma_start(h2_rows, bass.IndirectOffsetOnAxis(idx[:, 2 + b:3 + b], 0), yb[:, b, :],
                                         None, bounds_check=T - 1, oob_is_err=False, compute_op=ALU.add)\
                    .then_inc(S("scattered"), 16)

            gather(0, 0)
            gather(1, 1)
            pool_.wait_ge(S("ends_ready"), 1)
            rounds = pool_.value_load(ends[0:1, E + 1:E + 2], min_val=0, max_val=MAXB // 2 - 2)
            pool_.wait_ge(S("xt_ready"), 1)
            gather(2, 0)
            pool_.wait_ge(S("xt_ready"), 2)
            gather(3, 1)
            pool_.wait_ge(S("h2_stored"), 1)
            for k in range(2):
                pool_.wait_ge(S("xt_ready"), 3 + k)
                gather(4 + k, k)
                scatter(k, k, k == 0)
            with pool_.Fori(1, pool_.snap(rounds + 1)) as m:
                for k in range(2):
                    t = 2 * m + (1 + k)
                    pool_.wait_ge(S("xt_ready"), t + 2)
                    gather(t + 3, k)
                    scatter(t - 1, k)
            last = pool_.snap(2 * rounds + 3)
            scatter(last - 1, 0)
            scatter(last, 1)
            pool_.wait_ge(S("gathered0"), 8 * last + 24)
            pool_.wait_ge(S("gathered1"), 8 * last + 24)
            pool_.wait_ge(S("scattered"), 16 * last + 16)
            pool_.nop().then_inc(S("moe_done"), 1)

        @block.scalar
        def _(act):
            own = Order(act, S("act_own"))

            def f(out_, in_, func, **kw):
                return nc.scalar.activation(out_, in_, func, **kw)

            scratch = wy[:].rearrange("p r q s c -> p (r q s c)")
            for i in range(NT):
                act.wait_ge(S(f"ld_x{i // 2}") if i else S("ld_xfirst"), 16)
                own.add(f(scratch[:, 0:D], xin[i // 2][:, i % 2, :], ACT.Square, accum_out=stat[:, 0, i:i + 1]))
                own.wait()
                f(stat[:, 1, i:i + 1], stat[:, 0, i:i + 1], ACT.Sqrt, scale=1.0 / D, bias=EPS)\
                    .then_inc(S("root1"), 1)
            act.wait_ge(S("ld_ssm"), 48)
            f(sp[:, 0, :], par[:, 2, :], ACT.Exp).then_inc(S("param_act"), 1)
            act.wait_ge(S("param_dve"), 1)
            f(sp[:, 3, :], sp[:, 1, :], ACT.Exp)
            f(sp[:, 4, :], sp[:, 1, :], ACT.Exp, scale=float(STEP)).then_inc(S("param_act"), 1)
            act.wait_ge(S("param_dve"), 2)
            f(sp[:, 5:9, :], sp[:, 5:9, :], ACT.Sin).then_inc(S("param_act"), 1)
            for k in range(STEP):
                act.wait_ge(S("u_ready"), k + 1)
                f(ublk[:, :, k, :], psum[:, 2 + k % 2, 0:SSM].rearrange("p (g c) -> p g c", c=CH), ACT.Copy)\
                    .then_inc(S("u_taken"), 1)
            for q in range(4):
                act.wait_ge(S("Ut_ready"), q + 1)
                f(Ug[:, 4 * q:4 * q + 4, :], psum[:, 4 + q % 2, :], ACT.Copy).then_inc(S("Ug_taken"), 1)
            def take_qkv(i):
                b = 2 * (i % 2)
                act.wait_ge(S("qkv_ready"), i + 1)
                f(qk[:, i, 0:QW], psum[:, b, :], ACT.Copy)
                f(qk[:, i, QW:QW + KVW], psum[:, b + 1, 0:KVW], ACT.Copy)
                v_ = psum[:, b + 1, KVW:2 * KVW].rearrange("p (g d) -> p g d", g=KV)
                f(vaug[:, i, :, 0:HD], v_, ACT.Copy)
                f(vaug[:, i, :, 2 * HD:3 * HD], v_, ACT.Copy).then_inc(S("qkv_taken"), 1)

            def root_qk(half):
                ts = slice(NT // 2 * half, NT // 2 * half + NT // 2)
                act.wait_ge(S("qkss_ready"), half + 1)
                f(qkss[:, 1, ts], qkss[:, 0, ts], ACT.Sqrt, scale=1.0 / HD, bias=EPS).then_inc(S("qkroot"), 1)

            act.wait_ge(S("tile_set"), 3)
            take_qkv(0)
            take_qkv(1)
            act.wait_ge(S("resp_ready"), 1)
            f(resp, psum[:, 4:6, 0:SSM], ACT.Copy).then_inc(S("resp_taken"), 1)
            for k in range(8):
                d, r, q = k // 4, k // 2 % 2, k % 2
                act.wait_ge(S("ws_ready"), k + 1)
                f(ws[:, d, r, 4 * q:4 * q + 4, :], psum[:, 6 + k % 2, :], ACT.Copy).then_inc(S("ws_taken"), 1)
            for i in range(2, NT):
                take_qkv(i)
                if i == NT - 2:
                    root_qk(0)
            for q in range(4):
                act.wait_ge(S("y_ready"), q + 1)
                b = 2 * (q % 2)
                f(yg[:, 4 * q:4 * q + 4, :].rearrange("p (k h) b -> p h k b", h=2),
                  psum[:, b:b + 2, 0:2 * NBLK].rearrange("p h (k b) -> p h k b", k=2), ACT.Gelu_apprx_tanh)\
                    .then_inc(S("y_taken"), 1)
            root_qk(1)
            for q in range(4):
                act.wait_ge(S("yk_ready"), q + 1)
                o = ytok.rearrange("p s (g c) -> p g s c", c=CH)[:, 4 * q:4 * q + 4]
                i_ = psum[:, 2 + q % 2, :].rearrange("p (g s c) -> p g s c", g=4, s=STEP)
                f(o, i_, ACT.Copy).then_inc(S("yk_taken"), 1)
            for k in range(4):
                hh, q = k // 2, k % 2
                act.wait_ge(S("yT_ready"), k + 1)
                o = yT[:, hh, :].rearrange("p (b s) -> p s b", s=STEP)[:, 4 * q:4 * q + 4, :]
                i_ = psum[:, 4 + k, :].rearrange("p (s b) -> p s b", s=4)
                f(o, i_, ACT.Copy).then_inc(S("yT_taken"), 1)
            act.wait_ge(S("ld_glu"), 32)
            for k in range(4):
                co, th = k // 2, k % 2
                act.wait_ge(S("glu_ready"), k + 1)
                f(sglu[:, co, HALF * th:HALF * th + HALF], psum[:, k, :], ACT.Sigmoid, bias=bglu[:, co:co + 1])\
                    .then_inc(S("glu_sig"), 1)
            act.wait_ge(S("ssm_done"), 1)
            for n in range(3 * NT):
                i, part = n // 3, n % 3
                tok = slice(P * i, P * i + P)
                act.wait_ge(S("prep_ready"), n + 1)
                src = psum[:, n % 4, :].rearrange("p (h t) -> p h t", t=P)
                if part < 2:
                    f(QA[:, 4 * part:4 * part + 4, tok], src, ACT.Copy).then_inc(S("hi_done"), 1)
                else:
                    f(KB[0:HD, :, tok], src[0:HD, 0:KV, :], ACT.Copy)
                    f(KA[:, :, tok], src[:, 0:KV, :], ACT.Copy).then_inc(S("hi_done"), 1)
            for n in range(HEADS * 2 * NT):
                act.wait_ge(S("sT_ready"), n + 1)
                if n >= 3:
                    act.wait_ge(S("pv_done"), n - 2)
                f(pexp[:, n % 3, :], psum[:, 4 + n % 2, :], ACT.Exp).then_inc(S("exp_done"), 1)

            act.wait_ge(S("O_taken"), 2 * HEADS)

            def weights_hi(f_):
                act.wait_ge(S(f"ld_m{f_ % 2}"), 16 * (f_ // 2 + 1))
                f(wh[f_ % 2][:], wm[f_ % 2][:, 0:2 * NC], ACT.Copy).then_inc(S("split_hi"), 1)

            weights_hi(0)
            for c in range(NC):
                f(xh[:, c, :], xnT[:, c, :], ACT.Copy).then_inc(S("split_hi"), 1)
            weights_hi(1)
            for n in range(2 * NC):
                b = 4 * (n % 2)
                act.wait_ge(S("mrg_ready"), n + 1)
                if n >= 2:
                    act.wait_ge(S("mrg_taken"), n - 1)
                f(sg[:, n % 2, 0, :], psum[:, b, :], ACT.Sigmoid)
                f(sg[:, n % 2, 1, :], psum[:, b + 2, :], ACT.Sigmoid).then_inc(S("sg_done"), 1)
                if n % 2 == 0 and 2 <= n < 2 * NC - 2:
                    weights_hi(n // 2 + 1)
            act.wait_ge(S("mrg_taken"), 2 * NC)
            scratch = sg[:].rearrange("p a b n -> p (a b n)")
            for i in range(NT + 1):
                if i < NT:
                    act.wait_ge(S("h1_done"), i + 1)
                    own.wait()
                    own.add(f(scratch[:, 0:D], htile[:, i % 3, :], ACT.Square, accum_out=stat[:, 3, i:i + 1]))
                    own.wait()
                    f(stat[:, 4, i:i + 1], stat[:, 3, i:i + 1], ACT.Sqrt, scale=1.0 / D, bias=EPS)\
                        .then_inc(S("root2"), 1)
                if i >= 1:
                    for j in range(2):
                        n = 2 * (i - 1) + j
                        act.wait_ge(S("hnT_ready"), n + 1)
                        f(xnT[:, 4 * j:4 * j + 4, P * (i - 1):P * i],
                          psum[:, 4 + n % 3, :].rearrange("p (c t) -> p c t", c=4), ACT.Copy)\
                            .then_inc(S("hnT_taken"), 1)
            act.wait_ge(S("lg_ready"), 1)
            act.wait_ge(S("hnT_taken"), 2 * NT)
            act.wait_ge(S("h_stored"), NT)
            f(rt[:, 0].rearrange("p i e -> p (i e)"), psum[:, 7, :], ACT.Sigmoid).then_inc(S("sc_done"), 1)
            for i in range(NT):
                act.wait_ge(S("pT_ready"), i + 1)
                f(pT[:, :, P * i:P * i + P], psum[:, 1 + i % 2, 0:2 * P].rearrange("p (c t) -> p c t", c=2),
                  ACT.Copy).then_inc(S("pT_taken"), 1)
            for i in range(NT):
                b = 4 + 2 * (i % 2)
                act.wait_ge(S("prj_ready"), i + 1)
                if i >= 2:
                    act.wait_ge(S(f"st_prj{i % 2}"), 16 * (i // 2))
                f(prj[:, i % 2, :], psum[:, b:b + 2, :].rearrange("p k n -> p (k n)"), ACT.Copy)\
                    .then_inc(S("prj_done"), 1)
            for n in range(4):
                act.wait_ge(S("shgu_ready"), n + 1)
                if n >= 2:
                    act.wait_ge(S("sh_taken"), n - 1)
                f(shs[:, n % 2, :], psum[:, 4 + 2 * (n % 2), :], ACT.Silu).then_inc(S("shs_done"), 1)

            act.wait_ge(S("ends_ready"), 1)
            rounds = act.value_load(ends[0:1, E + 1:E + 2], min_val=0, max_val=MAXB // 2 - 2)

            def take_x(t, b, early=False):
                act.wait_ge(S("xt_ready"), t + 1)
                if not early:
                    act.wait_ge(S("gu_ready"), t - 1)
                f(xgT[:, b, 0:4, :].rearrange("p c s -> p (c s)"), psum[:, 0, :], ACT.Copy).then_inc(S("xa"), 1)

            def silu(t, b, early=False):
                act.wait_ge(S("gu_ready"), t + 1)
                if not early:
                    act.wait_ge(S("hid_ready"), t - 1)
                f(sgm[:, b, :], psum[:, 2 + b, 0:F], ACT.Silu).then_inc(S("sgm_ready"), 1)

            def take_y(t, b, early=False):
                act.wait_ge(S("y_made"), t + 2)
                if not early:
                    act.wait_ge(S("scattered"), 16 * t - 16)
                f(yb[:, b, 0:HALF], psum[:, 5, :], ACT.Copy, scale=tab[:, 1, bass.ds(t, 1)]).then_inc(S("ya"), 1)

            act.wait_ge(S("tab_ready"), 1)
            take_x(0, 0, True)
            take_x(1, 1, True)
            act.wait_ge(S("h2_stored"), 1)
            silu(0, 0, True)
            for k in range(2):
                t = 1 + k
                take_x(t + 1, k % 2, False)
                silu(t, (1 + k) % 2, t < 2)
                take_y(t - 1, k, True)
            with act.Fori(1, act.snap(rounds + 1)) as m:
                for k in range(2):
                    t = 2 * m + (1 + k)
                    take_x(t + 1, k)
                    silu(t, (1 + k) % 2)
                    take_y(t - 1, k)
            last = act.snap(2 * rounds + 3)
            silu(last, 1)
            take_y(last - 1, 0)
            take_y(last, 1)

            act.wait_ge(S("ld_last"), 16 * (E // RING + 2))
            for c in range(NC):
                f(wpg_hi[:, c, :], wpg[:, c, :], ACT.Copy).then_inc(S("split_hi"), 1)
            act.wait_ge(S("moe_done"), 1)

            def gate_of(i):
                b = 4 + 2 * (i % 2)
                act.wait_ge(S("pg_ready"), i + 1)
                if i >= 2:
                    act.wait_ge(S("out_done"), i - 1)
                f(pg[:, i % 2, :], psum[:, b:b + 2, :].rearrange("p k n -> p (k n)"), ACT.Sigmoid)\
                    .then_inc(S("pg_done"), 1)

            def norm_of(i):
                act.wait_ge(S("h3_done"), i + 1)
                own.add(f(prjt[:, i % 2, :], pg[:, i % 2, :], ACT.Square, accum_out=stat[:, 3, i:i + 1]))
                own.wait()
                f(stat[:, 4, i:i + 1], stat[:, 3, i:i + 1], ACT.Sqrt, scale=1.0 / D, bias=EPS)\
                    .then_inc(S("root4"), 1)

            for i in range(NT + 2):
                if i < NT:
                    act.wait_ge(S(f"ld_e{i % 5}"), 16 * (i // 5 + 1))
                    if i >= 2:
                        act.wait_ge(S("ht_ready"), 2 * (i - 1))
                    own.add(f(ht[:, i % 2, :], h2t[:, i % 5, :], ACT.Square, accum_out=stat[:, 0, i:i + 1]))
                    own.wait()
                    f(stat[:, 1, i:i + 1], stat[:, 0, i:i + 1], ACT.Sqrt, scale=1.0 / D, bias=EPS)\
                        .then_inc(S("root3"), 1)
                    for j in range(2):
                        n = 2 * i + j
                        act.wait_ge(S("ht_ready"), n + 1)
                        if i >= 2:
                            act.wait_ge(S("pg_ready"), i - 1)
                        f(hp_hi[:, i % 2, 4 * j:4 * j + 4, :], psum[:, n % 4, :].rearrange("p (c t) -> p c t", c=4),
                          ACT.Copy).then_inc(S("split_hi"), 1)
                if i >= 2:
                    if i >= 4:
                        act.wait_ge(S(f"st_out{i % 2}"), 16 * (i // 2 - 1))
                    gate_of(i - 2)
                    norm_of(i - 2)

        @block.vector
        def _(dve):
            own = Order(dve, S("dve_own"))
            v = nc.vector

            def tt(o, a, b, op):
                own.add(v.tensor_tensor(o, a, b, op))

            def tsc(o, a, s1, op0, s2=None, op1=None):
                own.add(v.tensor_scalar(o, a, s1, s2, op0, op1) if op1 is not None
                        else v.tensor_scalar(o, a, s1, None, op0))

            def cmul(o, a, b, t, neg_im=False):
                tt(o[0], a[0], b[0], ALU.mult)
                tt(t[0], a[1], b[1], ALU.mult)
                tt(o[1], a[0], b[1], ALU.mult)
                tt(t[1], a[1], b[0], ALU.mult)
                own.wait()
                tt(o[0], o[0], t[0], ALU.subtract)
                if neg_im:
                    own.add(v.scalar_tensor_tensor(out=o[1], in0=o[1], scalar=-1.0, in1=t[1],
                                                   op0=ALU.mult, op1=ALU.subtract))
                else:
                    tt(o[1], o[1], t[1], ALU.add)
                own.wait()

            dve.wait_ge(S("ld_const"), 32)

            def evac_x(i):
                for j in range(2):
                    dve.wait_ge(S("xT_ready"), 2 * i + j + 1)
                    v.tensor_tensor(xnT[:, 4 * j:4 * j + 4, P * i:P * i + P],
                                    psum[:, j, :].rearrange("p (c t) -> p c t", c=4),
                                    bcast(gcols[:, 4 * j:4 * j + 4], 2, P), ALU.mult)\
                        .then_inc(S("xT_taken"), 1)

            for i in range(NT):
                dve.wait_ge(S("root1"), i + 1)
                own.add(v.reciprocal(stat[:, 2, i:i + 1], stat[:, 1, i:i + 1]))
                own.wait()
                x_ = xin[i // 2][:, i % 2, :]
                v.tensor_scalar(x_, x_, stat[:, 2, i:i + 1], None, ALU.mult)\
                    .then_inc(S("xs_ready"), 1)
                if i >= 1:
                    evac_x(i - 1)
            evac_x(NT - 1)

            t4 = [tmp[:, k, :] for k in range(2)]
            DT, LR, LI, ER, R8, S1, S8, C1, C8, FR, FI, T1, T2, T3, T4 = range(15)

            def c_(k):
                return sp[:, k, :]

            dve.wait_ge(S("param_act"), 1)
            tt(c_(LR), par[:, 0, :], c_(DT), ALU.mult)
            tt(c_(LI), par[:, 1, :], c_(DT), ALU.mult)
            own.wait()
            v.engine_nop().then_inc(S("param_dve"), 1)
            tsc(c_(S1), c_(LI), 1.0, ALU.mult)
            tsc(c_(S8), c_(LI), float(STEP), ALU.mult)
            own.wait()
            ang = sp[:, S1:S8 + 1, :]
            turns = sp[:, T1:T2 + 1, :]
            tsc(turns, ang, 1.0 / TWO_PI, ALU.mult, ROUND, ALU.add)
            own.wait()
            tsc(turns, turns, ROUND, ALU.subtract)
            own.wait()
            part, rest = [], TWO_PI
            for bits in (8, 16):
                part.append(float(np.round(rest * 2.0 ** bits) / 2.0 ** bits))
                rest -= part[-1]
            for piece in part + [float(np.float32(rest))]:
                own.add(v.scalar_tensor_tensor(out=ang, in0=turns, scalar=-piece, in1=ang,
                                               op0=ALU.mult, op1=ALU.add))
                own.wait()
            tsc(ang, ang, float(np.pi), ALU.min, -float(np.pi), ALU.max)
            own.wait()
            cosa = sp[:, C1:C8 + 1, :]
            own.add(v.scalar_tensor_tensor(out=cosa, in0=ang, scalar=-1.0, in1=ang, op0=ALU.mult, op1=ALU.max))
            own.wait()
            tsc(cosa, cosa, -1.0, ALU.mult, float(np.pi / 2), ALU.add)
            own.wait()
            v.engine_nop().then_inc(S("param_dve"), 1)
            dve.wait_ge(S("param_act"), 3)
            own.add(v.memset(pw[:, 0, :, 0:1], 1.0))
            own.add(v.memset(pw[:, 1, :, 0:1], 0.0))
            tt(pw[:, 0, :, 1], c_(ER), c_(C1), ALU.mult)
            tt(pw[:, 1, :, 1], c_(ER), c_(S1), ALU.mult)
            own.wait()
            for lo, n, by in ((1, 1, 1), (1, 2, 2), (1, 4, 4)):
                cmul([pw[:, r, :, by + lo:by + lo + n] for r in range(2)],
                     [pw[:, r, :, lo:lo + n] for r in range(2)],
                     [pw[:, r, :, by:by + 1].to_broadcast([P, DP, n]) for r in range(2)],
                     [t4[k][:, 0:DP * n].rearrange("p (q n) -> p q n", n=n) for k in range(2)])
            tsc(c_(T3), pw[:, 0, :, 1], 1.0, ALU.subtract)
            tt(c_(T1), par[:, 0, :], par[:, 0, :], ALU.mult)
            tt(c_(T2), par[:, 1, :], par[:, 1, :], ALU.mult)
            own.wait()
            tt(c_(T1), c_(T1), c_(T2), ALU.add)
            own.wait()
            own.add(v.reciprocal(c_(T1), c_(T1)))
            tt(c_(FR), c_(T3), par[:, 0, :], ALU.mult)
            tt(c_(T2), pw[:, 1, :, 1], par[:, 1, :], ALU.mult)
            tt(c_(FI), pw[:, 1, :, 1], par[:, 0, :], ALU.mult)
            tt(c_(T4), c_(T3), par[:, 1, :], ALU.mult)
            own.wait()
            tt(c_(FR), c_(FR), c_(T2), ALU.add)
            tt(c_(FI), c_(FI), c_(T4), ALU.subtract)
            own.wait()
            tt(c_(FR), c_(FR), c_(T1), ALU.mult)
            tt(c_(FI), c_(FI), c_(T1), ALU.mult)
            own.wait()
            dve.wait_ge(S("ld_ssm"), 48)
            dve.wait_ge(S("tile_set"), 2)
            cmul([bb[:, 0], bb[:, 1]], [bc[:, 0], bc[:, 1]],
                 [bcast(c_(FR), 2, CH), bcast(c_(FI), 2, CH)],
                 [t4[k][:, 0:DP * CH].rearrange("p (q c) -> p q c", c=CH) for k in range(2)])
            shaped = [t4[k].rearrange("p (q s c) -> p q s c", s=STEP, c=CH) for k in range(2)]
            for d in range(DIRS):
                q = slice(PAIRS * d, PAIRS * d + PAIRS)
                powers = pw[:, :, q, STEP - 1::-1] if d == 0 else pw[:, :, q, 0:STEP]
                cmul([vp[:, r, q] for r in range(2)],
                     [bcast(bb[:, r, q, :], 2, STEP) for r in range(2)],
                     [bcast(powers[:, r], 3, CH) for r in range(2)], shaped)
            for gg in range(2):
                rows_ = slice(ST * gg, ST * gg + ST)
                own.add(v.tensor_copy(cblk[rows_, 0, :, gg, :], bc[rows_, 2]))
                tsc(cblk[rows_, 1, :, gg, :], bc[rows_, 3], -1.0, ALU.mult)
            own.add(v.tensor_copy(bbz[:, :, :, 1, :], bb[:, :, PAIRS:DP, :]))
            own.wait()
            v.engine_nop().then_inc(S("vp_ready"), 1)
            for d in range(DIRS):
                q = slice(PAIRS * d, PAIRS * d + PAIRS)
                powers = pw[:, :, q, 1:STEP + 1] if d == 0 else pw[:, :, q, STEP:0:-1]
                cmul([wy[:, r, q] for r in range(2)],
                     [bcast(bc[:, 2 + r, q, :], 2, STEP) for r in range(2)],
                     [bcast(powers[:, r], 3, CH) for r in range(2)], shaped, neg_im=True)

            dve.wait_ge(S("ws_ready"), 8)
            own.add(v.memset(rot[:, 0, :, 0:1], 1.0))
            own.add(v.memset(rot[:, 1, :, 0:1], 0.0))
            own.add(v.tensor_copy(rot[:, 0, :, 1], c_(C8)))
            own.add(v.tensor_copy(rot[:, 1, :, 1], c_(S8)))
            own.wait()
            n = 2
            while n < NBLK:
                cmul([c_(T3), c_(T4)], [rot[:, r, :, n // 2] for r in range(2)],
                     [rot[:, r, :, n // 2] for r in range(2)], [c_(T1), c_(T2)])
                cmul([rot[:, r, :, n:2 * n] for r in range(2)], [rot[:, r, :, 0:n] for r in range(2)],
                     [bcast(c_(T3), 2, n), bcast(c_(T4), 2, n)],
                     [t4[k][:, 0:DP * n].rearrange("p (q n) -> p q n", n=n) for k in range(2)])
                n *= 2
            dve.wait_ge(S("ld_ssm"), 48)
            dve.wait_ge(S("T0_ready"), 16 * (2 * STEP - 1))
            for g in range(GROUPS):
                own.add(v.scalar_tensor_tensor(out=t0[:, g, :].rearrange("p (t c) -> p t c", t=STEP),
                                               in0=ident.rearrange("p (t c) -> p t c", t=STEP),
                                               scalar=dskip[:, g:g + 1], in1=stage[:, :, CH * g:CH * g + CH],
                                               op0=ALU.mult, op1=ALU.add))
            own.wait()
            v.engine_nop().then_inc(S("T0_taken"), 1)
            for d in range(DIRS):
                dve.wait_ge(S("S_ready"), d + 1)
                co, si = (rot[:, r, PAIRS * d:PAIRS * d + PAIRS, :] for r in range(2))
                sre = psum[:, 4:6, :].rearrange("p k (j b) -> p (k j) b", b=NBLK)
                sim = psum[:, 6:8, :].rearrange("p k (j b) -> p (k j) b", b=NBLK)
                wre, wim = wrot[:, 0], wrot[:, 1]
                ta, tb = (t4[k].rearrange("p (j b) -> p j b", b=NBLK) for k in range(2))
                tt(wre, co, sre, ALU.mult)
                tt(ta, si, sim, ALU.mult)
                tt(wim, co, sim, ALU.mult)
                tt(tb, si, sre, ALU.mult)
                own.wait()
                v.engine_nop().then_inc(S("S_taken"), 1)
                tt(wre, wre, ta, ALU.add)
                tt(wim, wim, tb, ALU.subtract)
                own.wait()
                for r in range(2):
                    for j in range(PAIRS):
                        decay = sp[:, R8, PAIRS * d + j:PAIRS * d + j + 1].to_broadcast([P, NBLK])
                        own.add(v.tensor_tensor_scan(wrot[:, r, j, :], decay, wrot[:, r, j, :], 0.0,
                                                     ALU.mult, ALU.add))
                own.wait()
                keep = slice(0, NBLK - 1)
                xre, xim = (xs[:, d, r, :, 1:NBLK] for r in range(2))
                for r in range(2):
                    own.add(v.memset(xs[:, d, r, :, 0:1], 0.0))
                tt(xre, co[:, :, keep], wre[:, :, keep], ALU.mult)
                tt(ta[:, :, keep], si[:, :, keep], wim[:, :, keep], ALU.mult)
                tt(xim, co[:, :, keep], wim[:, :, keep], ALU.mult)
                tt(tb[:, :, keep], si[:, :, keep], wre[:, :, keep], ALU.mult)
                own.wait()
                tt(xre, xre, ta[:, :, keep], ALU.subtract)
                tt(xim, xim, tb[:, :, keep], ALU.add)
                own.wait()
                v.engine_nop().then_inc(S("X_ready"), 1)
            def heads(ap):
                return ap.rearrange("p (h d) -> p h d", d=HD)

            dve.wait_ge(S("ld_norms"), 32)
            cos_ = const[:, C_COS:C_COS + NT * HD].rearrange("p (i d) -> p i d", i=NT)
            sin_ = const[:, C_SIN:C_SIN + NT * HD].rearrange("p (i d) -> p i d", i=NT)
            for m in range(2):
                scale = HD ** -0.5 if m == 0 else 1.0
                w = nrmw[:, m, :]
                tt(rope[:, 2 * m], cos_, bcast(w, 1, NT), ALU.mult)
                for s_ in range(2):
                    o = rope[:, 2 * m + 1].rearrange("p i (a s f) -> p i a s f", a=2, s=2)[:, :, :, s_]
                    i0 = sin_.rearrange("p i (a s f) -> p i a s f", a=2, s=2)[:, :, :, s_]
                    i1 = w.rearrange("p (a s f) -> p a s f", a=2, s=2)[:, :, 1 - s_]
                    tt(o, i0, bcast(i1, 1, NT), ALU.mult)
                own.wait()
                if m == 0:
                    tsc(rope[:, 0], rope[:, 0], scale, ALU.mult)
                    tsc(rope[:, 1], rope[:, 1], scale, ALU.mult)
            for half in range(2):
                ts = slice(NT // 2 * half, NT // 2 * half + NT // 2)
                if half:
                    dve.wait_ge(S("qk_ready"), NT // 2)
                for i in range(NT // 2 * half, NT // 2 * half + NT // 2):
                    dve.wait_ge(S("qkv_taken"), i + 1)
                    tt(qtmp[:, i % 2, 0:QW + KVW], qk[:, i], qk[:, i], ALU.mult)
                    own.wait()
                    own.add(v.tensor_reduce(qkss[:, 0, i, :], heads(qtmp[:, i % 2, 0:QW + KVW]), AX_X, ALU.add))
                own.wait()
                v.engine_nop().then_inc(S("qkss_ready"), 1)
                dve.wait_ge(S("qkroot"), half + 1)
                own.add(v.reciprocal(qkss[:, 2, ts], qkss[:, 1, ts]))
                own.wait()
                for i in range(NT // 2 * half, NT // 2 * half + NT // 2):
                    if i >= 1:
                        dve.wait_ge(S("qk_ready"), i)
                    for m, (at, n) in enumerate(((0, HEADS), (QW, KV))):
                        src = qk[:, i, at:at + n * HD]
                        t1 = qtmp[:, 0, at:at + n * HD]
                        t2 = qtmp[:, 1, at:at + n * HD]
                        tt(heads(t1), heads(src), bcast(rope[:, 2 * m, i], 1, n), ALU.mult)
                        for s_ in range(2):
                            def part(ap, k):
                                return ap.rearrange("p (h a s f) -> p h a s f", a=2, s=2, f=HD // 4)[:, :, :, k]
                            sn = rope[:, 2 * m + 1, i].rearrange("p (a s f) -> p a s f", a=2, s=2)[:, :, s_]
                            tt(part(t2, s_), part(src, 1 - s_), bcast(sn, 1, n), ALU.mult)
                    own.wait()
                    both = qtmp[:, 0, 0:QW + KVW]
                    tt(both, both, qtmp[:, 1, 0:QW + KVW], ALU.add)
                    own.wait()
                    v.tensor_tensor(heads(qk[:, i]), heads(both), bcast(qkss[:, 2, i], 2, HD), ALU.mult)\
                        .then_inc(S("qk_ready"), 1)

            for k in range(4):
                co_, th = k // 2, k % 2
                cols = slice(HALF * th, HALF * th + HALF)
                dve.wait_ge(S("glu_sig"), k + 1)
                tt(ssmT[:, co_, cols], yT[:, co_, cols], sglu[:, co_, cols], ALU.mult)
            own.wait()
            v.engine_nop().then_inc(S("ssm_done"), 1)

            for n in range(3 * NT):
                i, part = n // 3, n % 3
                if part == 0:
                    for j in [0, 1] if i == 0 else [i + 1] if i + 1 < NT else []:
                        if j >= 2:
                            dve.wait_ge(S("prep_ready"), 3 * (j - 1) - 1)
                        v.tensor_copy(qkd[:, j % 2, 0:HEADS], bcast(heads(qk[:, j, 0:QW]), 2, 2))\
                            .then_inc(S("q_doubled"), 1)
                tok = slice(P * i, P * i + P)
                dve.wait_ge(S("hi_done"), n + 1)
                src = psum[:, n % 4, :].rearrange("p (h t) -> p h t", t=P)
                if part < 2:
                    hs = slice(4 * part, 4 * part + 4)
                    ins = v.tensor_tensor(QB[0:HD, hs, tok], src[0:HD], QA[0:HD, hs, tok].bitcast(F32),
                                          ALU.subtract)
                else:
                    ins = v.tensor_tensor(KA[HD:P, :, tok], src[HD:P, 0:KV, :], KA[HD:P, :, tok].bitcast(F32),
                                          ALU.subtract)
                ins.then_inc(S("prep_taken"), 1)

            def row_max(h, i):
                m = 9 * h + i
                dve.wait_ge(S("max_ready"), m + 1)
                b = 2 * (m % 2)
                if i < NT:
                    v.tensor_reduce(smax[:, h, i:i + 1], psum[:, b:b + 2, :].rearrange("p k n -> p (k n)"),
                                    AX_X, ALU.max).then_inc(S("max_taken"), 1)
                else:
                    v.tensor_scalar(smaxT[:, h, :], psum[0:NT, b, 0:P], -1.0, None, ALU.mult)\
                        .then_inc(S("max_taken"), 1)

            def finish_head(h, qh):
                n = 2 * h + qh
                dve.wait_ge(S("pv_done"), NT * (n + 1))
                a0, s0 = (0, HD) if h % 2 == 0 else (HD, 0)
                b = 6 + n % 2
                own.add(v.reciprocal(rsum[a0:a0 + HD, qh, :], psum[s0:s0 + HD, b, :]))
                own.wait()
                v.tensor_tensor(attnT[a0:a0 + HD, h // 2, HALF * qh:HALF * qh + HALF], psum[a0:a0 + HD, b, :],
                                rsum[a0:a0 + HD, qh, :], ALU.mult).then_inc(S("O_taken"), 1)

            for i in range(NT + 1):
                row_max(0, i)
            for h in range(HEADS):
                for k in range(2 * NT):
                    if k == 1 and h >= 1:
                        finish_head(h - 1, 1)
                    if k in MAX_STEPS and h + 1 < HEADS:
                        row_max(h + 1, MAX_STEPS.index(k))
                    if k == NT + 4:
                        finish_head(h, 0)
            finish_head(HEADS - 1, 1)

            def weights_lo(f_):
                w_ = wm[f_ % 2][:, 0:2 * NC]
                dve.wait_ge(S("split_hi"), split_no(f=f_))
                v.tensor_tensor(wl[f_ % 2][:], w_, wh[f_ % 2][:].bitcast(F32), ALU.subtract)\
                    .then_inc(S("split_lo"), 1)

            weights_lo(0)
            for c in range(NC):
                dve.wait_ge(S("split_hi"), split_no(c=c))
                v.tensor_tensor(xl[:, c, :], xnT[:, c, :], xh[:, c, :].bitcast(F32), ALU.subtract)\
                    .then_inc(S("split_lo"), 1)
            weights_lo(1)
            for n in range(2 * NC):
                b = 4 * (n % 2)
                s0, s1 = sg[:, n % 2, 0, :], sg[:, n % 2, 1, :]
                dve.wait_ge(S("sg_done"), n + 1)
                tt(s0, s0, psum[:, b + 1, :], ALU.mult)
                tt(s1, s1, psum[:, b + 3, :], ALU.mult)
                own.wait()
                v.tensor_tensor(mergedT[:, n // 2, HALF * (n % 2):HALF * (n % 2) + HALF], s0, s1, ALU.add)\
                    .then_inc(S("mrg_taken"), 1)
                if n % 2 == 0 and 2 <= n < 2 * NC - 2:
                    weights_lo(n // 2 + 1)
            dve.wait_ge(S("ld_out0"), 32)
            for i in range(NT + 1):
                if i >= 1:
                    k = i - 1
                    dve.wait_ge(S("root2"), k + 1)
                    own.add(v.reciprocal(stat[:, 5, k:k + 1], stat[:, 4, k:k + 1]))
                    own.wait()
                    if k >= 2:
                        dve.wait_ge(S("h_stored"), k - 1)
                        dve.wait_ge(S("hnT_ready"), 2 * (k - 1))
                    v.scalar_tensor_tensor(out=hntile[:, k % 2, :], in0=htile[:, k % 3, :],
                                           scalar=stat[:, 5, k:k + 1], in1=gffn[:], op0=ALU.mult,
                                           op1=ALU.mult).then_inc(S("hn_done"), 1)
                if i < NT:
                    b = 2 * (i % 2)
                    h = htile[:, i % 3, :]
                    dve.wait_ge(S(f"ld_h{i % 3}"), 16 * (i // 3 + 1))
                    dve.wait_ge(S("wo_ready"), i + 1)
                    v.tensor_tensor(h, h, psum[:, b:b + 2, :].rearrange("p k n -> p (k n)"), ALU.add)\
                        .then_inc(S("h1_done"), 1)

            dve.wait_ge(S("sc_done"), 1)
            dve.wait_ge(S("ld_router"), 32)
            SC, BIASED, MASKED, REPLACED, SEL, GATE, BEFORE, DEST, CUM, RANK = range(10)

            def r_(k):
                return rt[:, k]

            def byg(k):
                return rt[:, k].rearrange("p i (g e) -> p i g e", g=EG)

            tt(r_(BIASED), r_(SC), bcast(rbias[:], 1, NT), ALU.add)
            own.wait()
            best = cmp[:, 0].rearrange("p i (g k) -> p i g k", g=EG)
            for i in range(NT):
                for g in range(EG):
                    own.add(v.max(best[:, i, g, :], rt[:, BIASED, i, GE * g:GE * g + GE]))
            own.wait()
            tt(grp[:, 0], best[:, :, :, 0], best[:, :, :, 1], ALU.add)
            own.wait()
            mine = bcast(grp[:, 0], 3, EG)
            other = bcast(grp[:, 0], 2, EG)
            gt, eq = (cmp[:, k].rearrange("p i (g h) -> p i g h", g=EG) for k in (1, 2))
            tt(gt, other, mine, ALU.is_gt)
            tt(eq, other, mine, ALU.is_equal)
            own.wait()
            tt(cmp[:, 2], cmp[:, 2], bcast(const[:, C_LOW:C_LOW + EG * EG], 1, NT), ALU.mult)
            own.wait()
            tt(cmp[:, 1], cmp[:, 1], cmp[:, 2], ALU.add)
            own.wait()
            own.add(v.tensor_reduce(grp[:, 1], gt, AX_X, ALU.add))
            own.wait()
            tsc(grp[:, 2], grp[:, 1], float(TOPG), ALU.is_lt)
            own.wait()
            tsc(grp[:, 3], grp[:, 2], 1.0, ALU.subtract, 1e30, ALU.mult)
            tt(byg(MASKED), byg(BIASED), bcast(grp[:, 2], 3, GE), ALU.mult)
            own.wait()
            tt(byg(MASKED), byg(MASKED), bcast(grp[:, 3], 3, GE), ALU.add)
            own.wait()
            for i in range(NT):
                own.add(v.max(top[:, 0, i, :], rt[:, MASKED, i, :]))
            own.wait()
            for i in range(NT):
                own.add(v.match_replace(rt[:, REPLACED, i, :], top[:, 0, i, :], rt[:, MASKED, i, :], -3e38))
            own.wait()
            tt(r_(SEL), r_(MASKED), r_(REPLACED), ALU.not_equal)
            own.wait()
            tt(r_(GATE), r_(SC), r_(SEL), ALU.mult)
            own.add(v.memset(rt[:, BEFORE, 0, :], 0.0))
            own.wait()
            for i in range(1, NT):
                tt(rt[:, BEFORE, i, :], rt[:, BEFORE, i - 1, :], rt[:, SEL, i - 1, :], ALU.add)
                own.wait()
            tt(cnt[:, 0, :], rt[:, BEFORE, NT - 1, :], rt[:, SEL, NT - 1, :], ALU.add)
            own.wait()
            v.engine_nop().then_inc(S("sel_ready"), 1)
            own.add(v.tensor_reduce(top[:, 1, :, 0], r_(GATE), AX_X, ALU.add))
            own.wait()
            own.add(v.reciprocal(top[:, 1, :, 1], top[:, 1, :, 0]))
            own.wait()
            tsc(top[:, 1, :, 1], top[:, 1, :, 1], SCALE_ROUTED, ALU.mult)
            own.wait()
            tt(r_(GATE), r_(GATE), bcast(top[:, 1, :, 1], 2, E), ALU.mult)
            flat_ = [rt[:, k].rearrange("p i e -> p (i e)") for k in (CUM, SEL)]
            own.add(v.tensor_tensor_scan(flat_[0], const[:, C_ONE:C_ONE + 1].to_broadcast([P, NT * E]), flat_[1],
                                         0.0, ALU.mult, ALU.add))
            own.wait()
            for i in range(NT):
                own.add(v.scalar_tensor_tensor(out=rt[:, RANK, i, :], in0=rt[:, CUM, i, :], scalar=float(-TOPK * i),
                                               in1=rt[:, SEL, i, :], op0=ALU.add, op1=ALU.mult))
            dve.wait_ge(S("pos_ready"), 1)
            off = (SLOTS - 1) / (2 * SLOTS)
            tsc(cnt[:, 2, :], psum[:, 0, 0:E], 1.0 / SLOTS, ALU.mult, (SLOTS - 1) / SLOTS - off, ALU.add)
            pos = psum[:, 3, :].rearrange("p (i e) -> p i e", i=NT)
            own.wait()
            tsc(cnt[:, 2, :], cnt[:, 2, :], ROUND, ALU.add)
            own.wait()
            tsc(cnt[:, 2, :], cnt[:, 2, :], ROUND, ALU.subtract, 1.0, ALU.max)
            own.wait()
            own.add(v.tensor_tensor_scan(cnt[:, 3, :], const[:, C_ONE:C_ONE + 1].to_broadcast([P, E]), cnt[:, 2, :],
                                         0.0, ALU.mult, ALU.add))
            own.wait()
            tt(cnt[:, 4, :], cnt[:, 3, :], cnt[:, 2, :], ALU.subtract)
            own.wait()
            own.add(v.scalar_tensor_tensor(out=r_(DEST), in0=bcast(cnt[:, 4, :], 1, NT), scalar=float(SLOTS),
                                           in1=pos, op0=ALU.mult, op1=ALU.add))
            own.wait()
            v.engine_nop().then_inc(S("pos_taken"), 1)
            ranks = bcast(const[:, C_RANK:C_RANK + TOPK], 2, E)

            def hidden_shared(n):
                fc, th = n // 2, n % 2
                dve.wait_ge(S("shs_done"), n + 1)
                v.tensor_tensor(shT[:, fc, HALF * th:HALF * th + HALF], shs[:, n % 2, :],
                                psum[:, 5 + 2 * (n % 2), :], ALU.mult).then_inc(S("sh_taken"), 1)

            for i in range(NT):
                own.add(v.tensor_tensor(oh[:, 0], bcast(rt[:, RANK, i, :], 1, TOPK), ranks, ALU.is_equal))
                own.wait()
                for o, k in ((0, DEST), (1, GATE)):
                    tt(oh[:, 1], oh[:, 0], bcast(rt[:, k, i, :], 1, TOPK), ALU.mult)
                    own.wait()
                    own.add(v.tensor_reduce(dst[:, o, i, :], oh[:, 1], AX_X, ALU.add))
                    own.wait()
            tsc(dst[:, 2], dst[:, 0], 1.0 / SLOTS, ALU.mult, -off, ALU.add)
            own.wait()
            tsc(dst[:, 2], dst[:, 2], ROUND, ALU.add)
            own.wait()
            tsc(dst[:, 2], dst[:, 2], ROUND, ALU.subtract)
            own.wait()
            own.add(v.scalar_tensor_tensor(out=dst[:, 3], in0=dst[:, 2], scalar=float(-SLOTS), in1=dst[:, 0],
                                           op0=ALU.mult, op1=ALU.add))
            own.wait()
            v.engine_nop().then_inc(S("dest_ready"), 1)

            def block_rows():
                tsc(cnt[:, 5, :], cnt[:, 3, :], const[:, C_COL:C_COL + 1], ALU.is_le)
                own.wait()
                own.add(v.tensor_reduce(blk[:, 0:1], cnt[:, 5, :], AX_X, ALU.add))
                own.wait()
                tsc(blk[:, 0:1], blk[:, 0:1], float(E - 1), ALU.min)
                own.wait()
                tsc(blk[:, 1:2], blk[:, 0:1], 1.0 / RING, ALU.mult, -(RING - 1) / (2 * RING), ALU.add)
                own.wait()
                tsc(blk[:, 1:2], blk[:, 1:2], ROUND, ALU.add)
                own.wait()
                tsc(blk[:, 1:2], blk[:, 1:2], ROUND, ALU.subtract)
                own.wait()
                own.add(v.scalar_tensor_tensor(out=blk[:, 1:2], in0=blk[:, 1:2], scalar=float(-RING), in1=blk[:, 0:1],
                                               op0=ALU.mult, op1=ALU.add))
                tsc(cnt[:, 1, 0:1], cnt[:, 3, E - 1:E], 0.5, ALU.mult, 0.25, ALU.add)
                own.wait()
                v.engine_nop().then_inc(S("blk_ready"), 1)
                tsc(cnt[:, 1, 0:1], cnt[:, 1, 0:1], ROUND, ALU.add)
                own.wait()
                tsc(cnt[:, 1, 0:1], cnt[:, 1, 0:1], ROUND, ALU.subtract)
                own.wait()
                tsc(cnt[:, 1, 1:2], cnt[:, 1, 0:1], 2.0, ALU.subtract)
                own.wait()
                own.add(v.tensor_copy(ends[:, 0:E], cnt[:, 3, :]))
                own.add(v.tensor_copy(ends[:, E:E + 2], cnt[:, 1, 0:2]))

            for n in range(NT * TOPK):
                i, k = n // TOPK, n % TOPK
                if n == 10:
                    hidden_shared(0)
                if n == 14:
                    block_rows()
                if n == 17:
                    hidden_shared(1)
                if n == 43:
                    hidden_shared(2)
                if n >= 4:
                    dve.wait_ge(S("hot_used"), n - 3)
                tsc(blk_hot[:, n % 4, 0], const[:, C_IOTA:C_IOTA + P], dst[:, 2, i, k:k + 1], ALU.is_equal,
                    const[:, C_TOK + i:C_TOK + i + 1], ALU.mult)
                v.tensor_scalar(blk_hot[:, n % 4, 1], const[:, C_IOTA:C_IOTA + P], dst[:, 2, i, k:k + 1],
                                dst[:, 1, i, k:k + 1], ALU.is_equal, ALU.mult).then_inc(S("blk_hot"), 1)
            hidden_shared(3)
            dve.wait_ge(S("hot_used"), NT * TOPK)
            tsc(tab[:, 0, 0:MAXB], psum[:, 2, 0:MAXB], float(SKIP), ALU.add)
            own.add(v.tensor_copy(tab[:, 1, 0:MAXB], psum[:, 2, MAXB:2 * MAXB]))
            own.wait()
            v.engine_nop().then_inc(S("tab_ready"), 1)
            dve.wait_ge(S("rows_ready"), 1)
            own.add(v.tensor_copy(rows[0:2, 0:MAXB], psum[0:2, 3, 0:MAXB]))
            own.wait()
            v.engine_nop().then_inc(S("ends_ready"), 1)
            for i in range(NT):
                b = 2 * (i % 2)
                h = h1p[i // 2 % 2][:, i % 2, :]
                dve.wait_ge(S(f"ld_g{i // 2 % 2}"), 16 * (i // 4 + 1))
                dve.wait_ge(S("shd_ready"), i + 1)
                v.tensor_tensor(h, h,
                                psum[:, b:b + 2, :].rearrange("p k n -> p (k n)"), ALU.add)\
                    .then_inc(S("acc_done"), 1)

            rounds = dve.value_load(ends[0:1, E + 1:E + 2], min_val=0, max_val=MAXB // 2 - 2)

            def take_x(t, b, early=False):
                dve.wait_ge(S("xt_ready"), t + 1)
                if not early:
                    dve.wait_ge(S("gu_ready"), t - 1)
                v.tensor_copy(xgT[:, b, 4:8, :].rearrange("p c s -> p (c s)"), psum[:, 1, :]).then_inc(S("xd"), 1)

            def hidden(t, b, early=False):
                dve.wait_ge(S("sgm_ready"), t + 1)
                if not early:
                    dve.wait_ge(S("hT_ready"), t - 1)
                v.tensor_tensor(hid[:, b, :], sgm[:, b, :], psum[:, 2 + b, F:2 * F], ALU.mult)\
                    .then_inc(S("hid_ready"), 1)

            def take_h(t, b, early=False):
                dve.wait_ge(S("hT_ready"), t + 1)
                if not early:
                    dve.wait_ge(S("y_made"), t)
                v.tensor_copy(hidT[:, b, :], psum[:, 4, 0:SLOTS]).then_inc(S("hT_taken"), 1)

            def take_y(t, b, early=False):
                dve.wait_ge(S("y_made"), t + 2)
                if not early:
                    dve.wait_ge(S("scattered"), 16 * t - 16)
                v.tensor_scalar(yb[:, b, HALF:D], psum[:, 6, :], tab[:, 1, bass.ds(t, 1)], None, ALU.mult)\
                    .then_inc(S("yd"), 1)

            take_x(0, 0, True)
            take_x(1, 1, True)
            dve.wait_ge(S("h2_stored"), 1)
            hidden(0, 0, True)
            for k in range(2):
                t = 1 + k
                take_x(t + 1, k % 2)
                take_h(t - 1, k, True)
                hidden(t, (1 + k) % 2, t < 2)
                take_y(t - 1, k, True)
            with dve.Fori(1, dve.snap(rounds + 1)) as m:
                for k in range(2):
                    t = 2 * m + (1 + k)
                    take_x(t + 1, k)
                    take_h(t - 1, k)
                    hidden(t, (1 + k) % 2)
                    take_y(t - 1, k)
            last = dve.snap(2 * rounds + 3)
            take_h(last - 1, 0)
            hidden(last, 1)
            take_y(last - 1, 0)
            take_h(last, 1)
            take_y(last, 1)

            for c in range(NC):
                dve.wait_ge(S("split_hi"), GATE_SPLITS + c + 1)
                v.tensor_tensor(wpg_lo[:, c, :], wpg[:, c, :], wpg_hi[:, c, :].bitcast(F32), ALU.subtract)\
                    .then_inc(S("split_lo"), 1)
            dve.wait_ge(S("moe_done"), 1)

            def evac_h(i):
                for j in range(2):
                    n = 2 * i + j
                    dve.wait_ge(S("split_hi"), GATE_SPLITS + NC + n + 1)
                    v.tensor_tensor(hp_lo[:, i % 2, 4 * j:4 * j + 4, :],
                                    psum[:, n % 4, :].rearrange("p (c t) -> p c t", c=4),
                                    hp_hi[:, i % 2, 4 * j:4 * j + 4, :].bitcast(F32), ALU.subtract)\
                        .then_inc(S("split_lo"), 1)

            def finish(i):
                dve.wait_ge(S("pg_done"), i + 1)
                dve.wait_ge(S(f"ld_j{i % 2}"), 16 * (i // 2 + 1))
                g = pg[:, i % 2, :]
                tt(g, g, prjt[:, i % 2, :], ALU.mult)
                own.wait()
                v.tensor_tensor(g, g, h2t[:, i % 5, :], ALU.add).then_inc(S("h3_done"), 1)
                dve.wait_ge(S("root4"), i + 1)
                own.add(v.reciprocal(stat[:, 5, i:i + 1], stat[:, 4, i:i + 1]))
                own.wait()
                v.scalar_tensor_tensor(out=g, in0=g, scalar=stat[:, 5, i:i + 1], in1=gfin[:],
                                       op0=ALU.mult, op1=ALU.mult).then_inc(S("out_done"), 1)

            for i in range(NT + 2):
                if i < NT:
                    dve.wait_ge(S("root3"), i + 1)
                    own.add(v.reciprocal(stat[:, 2, i:i + 1], stat[:, 1, i:i + 1]))
                    own.wait()
                    v.scalar_tensor_tensor(out=ht[:, i % 2, :], in0=h2t[:, i % 5, :], scalar=stat[:, 2, i:i + 1],
                                           in1=gple[:], op0=ALU.mult, op1=ALU.mult)\
                        .then_inc(S("hs_ready"), 1)
                    evac_h(i)
                if i >= 2:
                    finish(i - 2)

        @block.tensor
        def _(pe):
            mm = nc.tensor.matmul
            tr = nc.tensor.transpose

            pe.wait_ge(S("ld_const"), 32)
            for i in range(NT):
                pe.wait_ge(S("xs_ready"), i + 1)
                for j in range(2):
                    if i >= 1:
                        pe.wait_ge(S("xT_taken"), 2 * (i - 1) + j + 1)
                    for c in range(4):
                        at = P * (4 * j + c)
                        ins = tr(psum[:, j, P * c:P * c + P], xin[i // 2][:, i % 2, at:at + P], ident)
                    ins.then_inc(S("xT_ready"), 1)
            pe.wait_ge(S("xT_taken"), 2 * NT)
            pe.wait_ge(S("ld_wu"), 16)
            for k in range(STEP):
                if k >= 2:
                    pe.wait_ge(S("u_taken"), k - 1)
                for c in range(NC):
                    ins = mm(psum[:, 2 + k % 2, 0:SSM], xnT[:, c, k::STEP], wu[:, c, :],
                             start=(c == 0), stop=(c == NC - 1))
                ins.then_inc(S("u_ready"), 1)
            pe.wait_ge(S("u_taken"), STEP)
            for q in range(4):
                if q >= 2:
                    pe.wait_ge(S("Ug_taken"), q - 1)
                for g in range(4):
                    ins = tr(psum[:, 4 + q % 2, P * g:P * g + P],
                             ublk[:, 4 * q + g].rearrange("p s c -> p (s c)"), ident)
                ins.then_inc(S("Ut_ready"), 1)
            def project(i):
                b = 2 * (i % 2)
                if i >= 2:
                    pe.wait_ge(S("qkv_taken"), i - 1)
                for at, n, bank in ((0, QW, b), (QW, 2 * KVW, b + 1)):
                    for c in range(NC):
                        ins = mm(psum[:, bank, 0:n], xnT[:, c, P * i:P * i + P], wqkv[:, c, at:at + n],
                                 start=(c == 0), stop=(c == NC - 1))
                ins.then_inc(S("qkv_ready"), 1)
            pe.wait_ge(S("ld_wqkv"), 16)
            project(0)
            project(1)
            pe.wait_ge(S("vp_ready"), 1)
            pe.wait_ge(S("Ug_taken"), 4)
            for j in range(PAIRS):
                cols = slice(2 * CH * j, 2 * CH * j + 2 * CH)
                mm(psum[:, 4, cols], vp[:, 0, j], cblk[:, 0, j], start=True, stop=False)
                for r in range(2):
                    mm(psum[P - 2 * CH:P, 4, cols], bbz[:, r, j], cblk[:, r, PAIRS + j], start=False, stop=False)
                mm(psum[:, 4, cols], vp[:, 1, j], cblk[:, 1, j], start=False, stop=True)
                for r in range(2):
                    ins = mm(psum[:, 5, cols], vp[:, r, PAIRS + j], cblk[:, r, PAIRS + j], start=(r == 0),
                             stop=(r == 1))
            ins.then_inc(S("resp_ready"), 1)
            for k in range(8):
                d, r, q = k // 4, k // 2 % 2, k % 2
                if k >= 2:
                    pe.wait_ge(S("ws_taken"), k - 1)
                for j in range(4):
                    ins = tr(psum[:, 6 + k % 2, P * j:P * j + P],
                             vp[:, r, PAIRS * d + 4 * q + j], ident)
                ins.then_inc(S("ws_ready"), 1)
            pe.wait_ge(S("resp_taken"), 1)
            pe.wait_ge(S("ws_taken"), 8)
            for d in range(DIRS):
                if d:
                    pe.wait_ge(S("S_taken"), d)
                for r in range(2):
                    for j in range(PAIRS):
                        for gg in range(2):
                            u_ = Ug[:, 2 * j + gg, :] if d == 0 else Ug[:, 2 * j + gg, ::-1]
                            ins = mm(psum[ST * gg:ST * gg + ST, 4 + 2 * r + j // 4, P * (j % 4):P * (j % 4) + P],
                                     ws[:, d, r, j, ST * gg:ST * gg + ST], u_, start=True, stop=True)
                ins.then_inc(S("S_ready"), 1)
                for i in range(2 + 3 * d, 5 + 3 * d):
                    project(i)
            pe.wait_ge(S("qkv_taken"), NT)
            pe.wait_ge(S("X_ready"), DIRS)
            pe.wait_ge(S("T0_taken"), 1)
            for q in range(4):
                if q >= 2:
                    pe.wait_ge(S("y_taken"), q - 1)
                for gi in range(4):
                    g = 4 * q + gi
                    j, gg = g // 2, g % 2
                    rows_ = slice(ST * gg, ST * gg + ST)
                    o = psum[:, 2 * (q % 2) + gg, P * (gi // 2):P * (gi // 2) + P]
                    mm(o, t0[:, g, :], Ug[:, g, :], start=True, stop=False)
                    for d in range(DIRS):
                        for r in range(2):
                            x_ = xs[rows_, d, r, j, :] if d == 0 else xs[rows_, d, r, j, ::-1]
                            ins = mm(o, wy[rows_, r, PAIRS * d + j], x_, start=False, stop=(d == 1 and r == 1))
                ins.then_inc(S("y_ready"), 1)
            for q in range(4):
                pe.wait_ge(S("y_taken"), 4)
                if q >= 2:
                    pe.wait_ge(S("yk_taken"), q - 1)
                for gi in range(4):
                    ins = tr(psum[:, 2 + q % 2, P * gi:P * gi + P], yg[:, 4 * q + gi, :], ident)
                ins.then_inc(S("yk_ready"), 1)
            pe.wait_ge(S("yk_taken"), 4)
            for k in range(4):
                hh, q = k // 2, k % 2
                for t in range(4):
                    ins = tr(psum[:, 4 + k, P * t:P * t + P], ytok[:, 4 * q + t, P * hh:P * hh + P], ident)
                ins.then_inc(S("yT_ready"), 1)
            pe.wait_ge(S("ld_glu"), 32)
            pe.wait_ge(S("yT_taken"), 4)
            for k in range(4):
                co, th = k // 2, k % 2
                for c in range(2):
                    ins = mm(psum[:, k, :], wglu[:, c, P * co:P * co + P], yT[:, c, HALF * th:HALF * th + HALF],
                             start=(c == 0), stop=(c == 1))
                ins.then_inc(S("glu_ready"), 1)
            pe.wait_ge(S("glu_sig"), 4)
            for n in range(3 * NT):
                i, part = n // 3, n % 3
                pe.wait_ge(S("q_doubled") if part < 2 else S("k_doubled"), i + 1)
                if n >= 4:
                    pe.wait_ge(S("prep_taken"), n - 3)
                at, count = (4 * part, 4) if part < 2 else (HEADS, KV)
                for h in range(count):
                    ins = tr(psum[:, n % 4, P * h:P * h + P],
                             qkd[:, i % 2, at + h].rearrange("p a d -> p (a d)"), ident)
                ins.then_inc(S("prep_ready"), 1)
            pe.wait_ge(S("prep_taken"), 3 * NT)
            pe.wait_ge(S("KB_ones"), 1)

            def max_scores(h, i):
                m = 9 * h + i
                b = 2 * (m % 2)
                if m >= 2:
                    pe.wait_ge(S("max_taken"), m - 1)
                if i < NT:
                    for kh in range(2):
                        ins = mm(psum[:, b + kh, :], QA[0:HD, h, P * i:P * i + P],
                                 KB[0:HD, h // REP, HALF * kh:HALF * kh + HALF], start=True, stop=True)
                else:
                    pe.wait_ge(S("max_taken"), m)
                    ins = tr(psum[0:NT, b, 0:P], smax[:, h, :], ident)
                ins.then_inc(S("max_ready"), 1)

            def attend(n):
                h, qh, j = n // (2 * NT), n // NT % 2, n % NT
                pe.wait_ge(S("exp_done"), n + 1)
                if j == 0 and 2 * h + qh >= 2:
                    pe.wait_ge(S("O_taken"), 2 * h + qh - 1)
                at = HD * (h % 2)
                ins = mm(psum[:, 6 + (2 * h + qh) % 2, :], vaug[:, j, h // REP, at:at + 2 * HD],
                         pexp[:, n % 3, :], start=(j == 0), stop=(j == NT - 1))
                ins.then_inc(S("pv_done"), 1)

            for i in range(NT + 1):
                max_scores(0, i)
            steps = HEADS * 2 * NT
            for n in range(steps):
                h, qh, j = n // (2 * NT), n // NT % 2, n % NT
                if n % (2 * NT) == 0:
                    pe.wait_ge(S(f"mrow{h % 2}"), 16 * (h // 2 + 1))
                if n >= 2:
                    pe.wait_ge(S("exp_done"), n - 1)
                o = psum[:, 4 + n % 2, :]
                cols = slice(HALF * qh, HALF * qh + HALF)
                keys = slice(P * j, P * j + P)
                mm(o, KA[:, h // REP, keys], QA[:, h, cols], start=True, stop=False)
                mm(o, KB[0:HD + 1, h // REP, keys], QB[0:HD + 1, h, cols], start=False, stop=True)\
                    .then_inc(S("sT_ready"), 1)
                if n >= 1:
                    attend(n - 1)
                k = n % (2 * NT)
                if k in MAX_STEPS and h + 1 < HEADS:
                    max_scores(h + 1, MAX_STEPS.index(k))
            attend(steps - 1)

            pe.wait_ge(S("max_taken"), 9 * HEADS)
            pe.wait_ge(S("O_taken"), 2 * HEADS)
            def ups(n):
                f_, th = n // 2, n % 2
                cols = slice(HALF * th, HALF * th + HALF)
                pe.wait_ge(S(f"ld_m{f_ % 2}"), 16 * (f_ // 2 + 1))
                if n >= 2:
                    pe.wait_ge(S("mrg_taken"), n - 1)
                for k, at, count, src in ((1, 16, 4, attnT), (3, 20, 2, ssmT)):
                    for c in range(count):
                        mm(psum[:, 4 * (n % 2) + k, :], wm[f_ % 2][:, at + c, :], src[:, c, cols],
                           start=(c == 0), stop=(c == count - 1))

            def gates(n):
                f_, th = n // 2, n % 2
                cols = slice(HALF * th, HALF * th + HALF)
                pe.wait_ge(S("split_lo"), split_no(f=f_))
                for k in range(2):
                    for c in range(NC):
                        if n == 0 and k == 0:
                            pe.wait_ge(S("split_lo"), split_no(c=c))
                        o = psum[:, 4 * (n % 2) + 2 * k, :]
                        w_hi, w_lo = wh[f_ % 2][:, NC * k + c, :], wl[f_ % 2][:, NC * k + c, :]
                        mm(o, w_hi, xh[:, c, cols], start=(c == 0), stop=False)
                        mm(o, w_lo, xh[:, c, cols], start=False, stop=False)
                        ins = mm(o, w_hi, xl[:, c, cols], start=False, stop=(c == NC - 1))
                ins.then_inc(S("mrg_ready"), 1)

            for n in (0, 1):
                ups(n)
            for n in range(2 * NC):
                if n >= 2:
                    ups(n)
                gates(n)
            pe.wait_ge(S("mrg_taken"), 2 * NC)
            pe.wait_ge(S("ld_router"), 32)
            for i in range(NT + 2):
                if i < NT:
                    if i >= 2:
                        pe.wait_ge(S("h1_done"), i - 1)
                    for c in range(NC):
                        for k, (lo, hi) in enumerate(WOUT_PARTS):
                            if i == 0 and c == lo:
                                pe.wait_ge(S(f"ld_out{k}"), 16 if k else 32)
                        for nh in range(2):
                            ins = mm(psum[:, 2 * (i % 2) + nh, :], mergedT[:, c, P * i:P * i + P],
                                     wout[:, c, HALF * nh:HALF * nh + HALF], start=(c == 0), stop=(c == NC - 1))
                    ins.then_inc(S("wo_ready"), 1)
                if 1 <= i <= NT:
                    pe.wait_ge(S("hn_done"), i)
                    for j in range(2):
                        n = 2 * (i - 1) + j
                        if n >= 3:
                            pe.wait_ge(S("hnT_taken"), n - 2)
                        for c in range(4):
                            at = P * (4 * j + c)
                            ins = tr(psum[:, 4 + n % 3, P * c:P * c + P], hntile[:, (i - 1) % 2, at:at + P], ident)
                        ins.then_inc(S("hnT_ready"), 1)
                if i >= 2:
                    pe.wait_ge(S("hnT_taken"), 2 * (i - 1))
                    k = i - 2
                    for c in range(NC):
                        ins = mm(psum[:, 7, E * k:E * k + E], xnT[:, c, P * k:P * k + P], wrt[:, c, :],
                                 start=(c == 0), stop=(c == NC - 1))
            ins.then_inc(S("lg_ready"), 1)
            pe.wait_ge(S("h1_done"), NT)
            pe.wait_ge(S("ld_p"), 32)
            for i in range(NT):
                if i >= 2:
                    pe.wait_ge(S("pT_taken"), i - 1)
                for c in range(2):
                    ins = tr(psum[:, 1 + i % 2, P * c:P * c + P], ptok[:, i, P * c:P * c + P], ident)
                ins.then_inc(S("pT_ready"), 1)
            for i in range(NT):
                if i == 4:
                    pe.wait_ge(S("sel_ready"), 1)
                    mm(psum[:, 3, :], const[:, C_TRI:C_TRI + P], rt[:, 4].rearrange("p i e -> p (i e)"),
                       start=True, stop=False)
                    mm(psum[:, 3, :], ones, rt[:, 6].rearrange("p i e -> p (i e)"), start=False, stop=True)
                    mm(psum[:, 0, 0:E], ones, cnt[:, 0, :], start=True, stop=True).then_inc(S("pos_ready"), 1)
                pe.wait_ge(S("pT_taken"), i + 1)
                if i >= 2:
                    pe.wait_ge(S("prj_done"), i - 1)
                for nh in range(2):
                    for c in range(2):
                        ins = mm(psum[:, 4 + 2 * (i % 2) + nh, :], pT[:, c, P * i:P * i + P],
                                 wpp[:, c, HALF * nh:HALF * nh + HALF], start=(c == 0), stop=(c == 1))
                ins.then_inc(S("prj_ready"), 1)
            pairs = NT * TOPK

            def fill_slots(lo, hi):
                for n in range(lo, hi):
                    pe.wait_ge(S("slot_hot"), n + 1)
                    pe.wait_ge(S("blk_hot"), n + 1)
                    mm(psum[:, 2, 0:2 * MAXB], slot_hot[:, n % 4, :],
                       blk_hot[:, n % 4].rearrange("p v b -> p (v b)"), start=(n == 0), stop=(n == pairs - 1))\
                        .then_inc(S("hot_used"), 1)

            pe.wait_ge(S("ld_wsh"), 32)
            pe.wait_ge(S("prj_done"), NT)
            done = 0
            for n in range(4):
                fc, th = n // 2, n % 2
                if n >= 2:
                    pe.wait_ge(S("sh_taken"), n - 1)
                for k in range(2):
                    for c in range(NC):
                        ins = mm(psum[:, 4 + 2 * (n % 2) + k, :], wsg[:, c, k, P * fc:P * fc + P],
                                 xnT[:, c, HALF * th:HALF * th + HALF], start=(c == 0), stop=(c == NC - 1))
                        if k == 1 and c == NC - 1:
                            ins.then_inc(S("shgu_ready"), 1)
                        if 2 * n + k >= 3:
                            upto = pairs * (NC * (2 * n + k - 3) + c + 1) // (5 * NC)
                            fill_slots(done, upto)
                            done = upto
            pe.wait_ge(S("blk_ready"), 1)
            pe.wait_ge(S("pos_taken"), 1)
            tr(psum[0:2, 3, 0:P], blk[:, 0:2], ident).then_inc(S("rows_ready"), 1)
            pe.wait_ge(S("ends_ready"), 1)
            pe.wait_ge(S("tab_ready"), 1)
            pe.wait_ge(S("sh_taken"), 4)
            for i in range(NT):
                if i >= 2:
                    pe.wait_ge(S("acc_done"), i - 1)
                for nh in range(2):
                    for c in range(2):
                        ins = mm(psum[:, 2 * (i % 2) + nh, :], shT[:, c, P * i:P * i + P],
                                 wsd[:, c, HALF * nh:HALF * nh + HALF], start=(c == 0), stop=(c == 1))
                ins.then_inc(S("shd_ready"), 1)

            pe.wait_ge(S("acc_done"), NT)
            rounds = pe.value_load(ends[0:1, E + 1:E + 2], min_val=0, max_val=MAXB // 2 - 2)

            def turn_x(t, b, count, early=False):
                pe.wait_ge(S(f"gathered{b}"), 16 * count + 16)
                if not early:
                    pe.wait_ge(S("xa"), t)
                    pe.wait_ge(S("xd"), t)
                for c in range(NC):
                    ins = tr(psum[:, c // 4, P * (c % 4):P * (c % 4) + P], xg[:, b, P * c:P * c + P], ident)
                ins.then_inc(S("xt_ready"), 1)

            def gate_up(t, b, early=False):
                expert = pe.value_load(rows[0:1, bass.ds(t, 1)], min_val=0, max_val=E - 1)
                slot = pe.value_load(rows[1:2, bass.ds(t, 1)], min_val=0, max_val=RING - 1)
                pe.wait_ge(S("w_ready"), expert + 1)
                pe.wait_ge(S("xa"), t + 1)
                pe.wait_ge(S("xd"), t + 1)
                if not early:
                    pe.wait_ge(S("hid_ready"), t - 1)
                for c in range(NC):
                    ins = mm(psum[:, 2 + b, 0:2 * F], xgT[:, b, c, :],
                             wexp[:, bass.ds(slot, 1), 2 * F * c:2 * F * c + 2 * F].rearrange("p a n -> p (a n)"),
                             start=(c == 0), stop=(c == NC - 1))
                ins.then_inc(S("gu_ready"), 1)

            def turn_h(t, b, early=False):
                pe.wait_ge(S("hid_ready"), t + 1)
                if not early:
                    pe.wait_ge(S("hT_taken"), t)
                tr(psum[:, 4, 0:SLOTS], hid[:, b, :], ident).then_inc(S("hT_ready"), 1)

            def down(t, b, early=False):
                slot = pe.value_load(rows[1:2, bass.ds(t, 1)], min_val=0, max_val=RING - 1)
                pe.wait_ge(S("hT_taken"), t + 1)
                if not early:
                    pe.wait_ge(S("ya"), t)
                    pe.wait_ge(S("yd"), t)
                for nh in range(2):
                    at = NC * 2 * F + HALF * nh
                    ins = mm(psum[:, 5 + nh, :], hidT[:, b, :],
                             wexp[:, bass.ds(slot, 1), at:at + HALF].rearrange("p a n -> p (a n)"),
                             start=True, stop=True)
                ins.then_inc(S("y_made"), 1)

            pe.nop().then_inc(S("y_made"), 1)
            turn_x(0, 0, 0, True)
            turn_x(1, 1, 0)
            gate_up(0, 0, True)
            for k in range(2):
                t = 1 + k
                turn_x(t + 1, k, 1)
                turn_h(t - 1, k, t == 1)
                gate_up(t, (1 + k) % 2, t < 2)
                down(t - 1, k, t == 1)
            with pe.Fori(1, pe.snap(rounds + 1)) as m:
                for k in range(2):
                    t = 2 * m + (1 + k)
                    turn_x(t + 1, k, m + 1)
                    turn_h(t - 1, k)
                    gate_up(t, (1 + k) % 2)
                    down(t - 1, k)
            last = pe.snap(2 * rounds + 3)
            turn_h(last - 1, 0)
            gate_up(last, 1)
            down(last - 1, 0)
            turn_h(last, 1)
            down(last, 1)

            pe.wait_ge(S("moe_done"), 1)
            for i in range(NT + 1):
                if i < NT:
                    pe.wait_ge(S("hs_ready"), i + 1)
                    for j in range(2):
                        n = 2 * i + j
                        if n >= 4:
                            pe.wait_ge(S("split_lo"), GATE_SPLITS + NC + n - 3)
                        for c in range(4):
                            at = P * (4 * j + c)
                            ins = tr(psum[:, n % 4, P * c:P * c + P], ht[:, i % 2, at:at + P], ident)
                        ins.then_inc(S("ht_ready"), 1)
                if i >= 1:
                    k = i - 1
                    pe.wait_ge(S("split_lo"), GATE_SPLITS + NC + 2 * k + 2)
                    if k >= 2:
                        pe.wait_ge(S("pg_done"), k - 1)
                    for nh in range(2):
                        cols = slice(HALF * nh, HALF * nh + HALF)
                        for c in range(NC):
                            o = psum[:, 4 + 2 * (k % 2) + nh, :]
                            hi, lo = hp_hi[:, k % 2, c, :], hp_lo[:, k % 2, c, :]
                            mm(o, hi, wpg_hi[:, c, cols], start=(c == 0), stop=False)
                            mm(o, hi, wpg_lo[:, c, cols], start=False, stop=False)
                            ins = mm(o, lo, wpg_hi[:, c, cols], start=False, stop=(c == NC - 1))
                    ins.then_inc(S("pg_ready"), 1)


def constants():
    c = np.zeros((P, C_END), np.float32)
    c[:, C_ID:C_ID + P] = np.eye(P)
    c[:, C_TRI:C_TRI + P] = np.triu(np.ones((P, P)), 1)
    t = np.arange(T)
    inv = (10000.0 ** (-np.arange(0, HD // 2, 2, dtype=np.float32) / (HD // 2))).astype(np.float32)
    ang = np.stack([(t // GRID_W)[:, None] * inv, (t % GRID_W)[:, None] * inv], 1).astype(np.float32)
    ang = ang.astype(np.float64)
    cos = np.stack([np.cos(ang), np.cos(ang)], 2).reshape(NT, P, HD)
    sin = np.stack([-np.sin(ang), np.sin(ang)], 2).reshape(NT, P, HD)
    c[:, C_COS:C_COS + NT * HD] = cos.transpose(1, 0, 2).reshape(P, -1)
    c[:, C_SIN:C_SIN + NT * HD] = sin.transpose(1, 0, 2).reshape(P, -1)
    c[:, C_TOK:C_TOK + NT] = t.reshape(NT, P).T - SKIP
    c[:, C_COL] = np.arange(P)
    c[:, C_LOW:C_LOW + EG * EG] = np.tril(np.ones((EG, EG)), -1).reshape(-1)
    c[:, C_RANK:C_RANK + TOPK] = np.arange(1, TOPK + 1)
    c[:, C_ONE:C_ONE + P] = 1.0
    c[:, C_IOTA:C_IOTA + P] = np.arange(P)
    return c


def layout(a):
    a = {k: np.asarray(v) for k, v in a.items()}

    def cols(g):
        return g.reshape(-1, P).T

    def states(v):
        v = v.reshape(DIRS, PAIRS, 2, ST, *v.shape[3:])
        return np.moveaxis(v, (2, 3, 0, 1), (0, 1, 2, 3)).reshape(P, DP, *v.shape[4:])

    log_dt = np.broadcast_to(a["log_dt"][0][:, :, None], (DIRS, GROUPS, ST))
    gate = a["w_exp_gate"][0].reshape(E, NC, P, F)
    up = a["w_exp_up"][0].reshape(E, NC, P, F)
    gu = np.stack([gate, up], 3).transpose(0, 2, 1, 3, 4).reshape(E, P, NC * 2 * F)

    def rows(w):
        return w.reshape(-1, P, w.shape[-1]).transpose(1, 0, 2)

    w_in = rows(a["w_in"][0])
    merge = np.concatenate([w_in[:, :, GATE_A:GATE_S], w_in[:, :, GATE_S:], rows(a["w_attn_up"][0]),
                            rows(a["w_ssm_up"][0])], 1)
    r = {
        "w_u": w_in[:, :, QW + 2 * KVW:GATE_A],
        "w_qkv": w_in[:, :, 0:QW + 2 * KVW],
        "w_merge": merge.reshape(P, -1, NC, P).transpose(2, 0, 1, 3),
        "w_sh_gate_up": np.stack([rows(a["w_sh_gate"][0]), rows(a["w_sh_up"][0])], 2),
        "const": constants(),
        "gcols": cols(a["g_mix"][0]),
        "ssm_par": np.stack([states(a["a_re"][0]), states(a["a_im"][0]), states(log_dt)], 1),
        "ssm_bc": np.stack([states(a["b_re"][0]), states(a["b_im"][0]),
                            states(a["c_re"][0].transpose(0, 1, 3, 2)),
                            states(a["c_im"][0].transpose(0, 1, 3, 2))], 1),
        "d_skip": np.broadcast_to(a["d_skip"][0].reshape(1, GROUPS, CH), (STEP, GROUPS, CH))
        .transpose(0, 2, 1).reshape(P, GROUPS),
        "b_glu": cols(a["b_glu"][0]),
        "w_ple_gate": a["w_ple_gate"][0].reshape(NC, P, 2, HALF).transpose(0, 2, 1, 3).reshape(2 * NC, P, HALF),
        "w_exp": np.concatenate([gu, a["w_exp_down"][0]], 2),
        "x": a["x"][0], "p": a["p"][0, 0], "g_final": a["g_final"],
    }
    for k in ("q_norm", "k_norm", "w_glu", "w_out", "g_ffn", "w_router",
              "router_bias", "w_sh_down", "g_ple", "w_ple_proj"):
        r[k] = a[k][0]
    return {k: np.ascontiguousarray(v) for k, v in r.items()}


def kernel(**inputs):
    import concourse.bacc as bacc
    from concourse.bass_utils import run_bass_kernel_spmd

    nc = bacc.Bacc("TRN2", target_bir_lowering=False, num_devices=1)
    arrays = {f"in_{k}": v for k, v in layout(inputs).items()}
    A = {k[3:]: nc.dram_tensor(k, v.shape, mybir.dt.from_np(v.dtype), kind="ExternalInput").ap()
         for k, v in arrays.items()}
    out = nc.dram_tensor("out", (T, D), F32, kind="ExternalOutput").ap()
    build(nc, A, out)
    r = run_bass_kernel_spmd(nc, [arrays], core_ids=[0])
    return r.results[0]["out"].reshape(1, T, D)
```
